# Optimizing a Trainium2 kernel written in Bass

```python
import jax, jax.numpy as jnp
from jax import lax
import numpy as np

D_MODEL = 1024
BATCH = 1
SEQ = 1024
DEPTH = 1
DEC_BATCH = 1
DEC_SEQ = 64
PAST_LEN = 512

CHUNK = 64
D_CONV = 1024
CONV_W = 3
N_HEADS = 16
N_KV_HEADS = 4
HEAD_DIM = 64
GQA_GROUP = N_HEADS // N_KV_HEADS
WINDOW = 128
WINDOW_CHUNKS = WINDOW // CHUNK
ROPE_THETA = 10000.0
ATTN_SCALE = HEAD_DIM ** -0.5
N_EXPERTS = 64
TOP_K = 8
N_EXPERT_GROUPS = 8
TOPK_GROUPS = 4
D_EXPERT = 256
D_SHARED = 256
ROUTED_SCALE = 2.5
DISPATCH_BLOCK = 128
EPS = 1e-6
Q_DIM = N_HEADS * HEAD_DIM
KV_DIM = N_KV_HEADS * HEAD_DIM
SPLITS = (D_CONV, D_CONV, D_CONV, Q_DIM, KV_DIM, KV_DIM, D_MODEL, D_MODEL)
D_IN = sum(SPLITS)

kernel_name = 'hybrid_stream_conv_swa_moe_step'

def rms_norm(x):
    xf = x.astype(jnp.float32)
    y = xf * lax.rsqrt(jnp.mean(xf * xf, axis=-1, keepdims=True) + EPS)
    return y.astype(x.dtype)

def rope(x, pos):
    half = HEAD_DIM // 2
    inv_freq = ROPE_THETA ** (-jnp.arange(half, dtype=jnp.float32) / half)
    ang = pos.astype(jnp.float32)[:, None] * inv_freq[None, :]
    cos = jnp.cos(ang)[:, None, :]
    sin = jnp.sin(ang)[:, None, :]
    xf = x.astype(jnp.float32)
    x1, x2 = xf[..., :half], xf[..., half:]
    return jnp.concatenate([x1 * cos - x2 * sin, x2 * cos + x1 * sin], axis=-1).astype(x.dtype)

def sink_softmax(scores, sinks):
    s = sinks.astype(jnp.float32).reshape(N_KV_HEADS, GQA_GROUP, 1, 1)
    m = jnp.maximum(jnp.max(scores, axis=-1, keepdims=True), s)
    e = jnp.exp(scores - m)
    z = jnp.sum(e, axis=-1, keepdims=True) + jnp.exp(s - m)
    return e / z

def band_attention(q, k, v, sinks):
    b, s = q.shape[:2]
    nc = s // CHUNK
    qc = q.reshape(b, nc, CHUNK, N_KV_HEADS, GQA_GROUP, HEAD_DIM)

    def band(t):
        tc = t.reshape(b, nc, CHUNK, N_KV_HEADS, HEAD_DIM)
        tp = jnp.pad(tc, ((0, 0), (WINDOW_CHUNKS, 0), (0, 0), (0, 0), (0, 0)))
        return jnp.concatenate([tp[:, j:j + nc] for j in range(WINDOW_CHUNKS + 1)], axis=2)

    kb, vb = band(k), band(v)
    band_len = (WINDOW_CHUNKS + 1) * CHUNK
    key_chunk = jnp.arange(nc)[:, None] + jnp.arange(band_len)[None, :] // CHUNK - WINDOW_CHUNKS
    valid = (key_chunk >= 0)[None, :, None, None, None, :]
    scores = jnp.einsum('bnqhgd,bnkhd->bnhgqk', qc, kb, preferred_element_type=jnp.float32) * ATTN_SCALE
    p = sink_softmax(jnp.where(valid, scores, -jnp.inf), sinks)
    o = jnp.einsum('bnhgqk,bnkhd->bnqhgd', p.astype(v.dtype), vb)
    return o.reshape(b, s, Q_DIM)

def cached_attention(q, k_all, v_all, sinks):
    b, t = q.shape[:2]
    qg = q.reshape(b, t, N_KV_HEADS, GQA_GROUP, HEAD_DIM)
    scores = jnp.einsum('bqhgd,bkhd->bhgqk', qg, k_all, preferred_element_type=jnp.float32) * ATTN_SCALE
    p = sink_softmax(scores, sinks)
    o = jnp.einsum('bhgqk,bkhd->bqhgd', p.astype(v_all.dtype), v_all)
    return o.reshape(b, t, Q_DIM)

def causal_conv(u_ext, w):
    t = u_ext.shape[1] - (CONV_W - 1)
    out = w[0] * u_ext[:, 0:t]
    for i in range(1, CONV_W):
        out = out + w[i] * u_ext[:, i:i + t]
    return out

def token_mixer(h, pos, conv_hist, k_hist, v_hist, w_in, w_conv, w_conv_out, w_attn_o, attn_sinks, w_mix_out):
    b, t = h.shape[:2]
    offsets = [int(o) for o in np.cumsum(SPLITS)[:-1]]
    gate_b, gate_c, x_conv, q, k, v, g_conv, g_attn = jnp.split(h @ w_in, offsets, axis=-1)
    u = gate_c * x_conv
    if conv_hist is None:
        u_ext = jnp.pad(u, ((0, 0), (CONV_W - 1, 0), (0, 0)))
    else:
        u_ext = jnp.concatenate([conv_hist.astype(u.dtype), u], axis=1)
    y_conv = (gate_b * causal_conv(u_ext, w_conv)) @ w_conv_out
    new_conv = u_ext[:, -(CONV_W - 1):]
    q = rope(q.reshape(b, t, N_HEADS, HEAD_DIM), pos)
    k = rope(k.reshape(b, t, N_KV_HEADS, HEAD_DIM), pos)
    v = v.reshape(b, t, N_KV_HEADS, HEAD_DIM)
    if k_hist is None:
        o = band_attention(q, k, v, attn_sinks)
        k_all, v_all = k, v
    else:
        k_all = jnp.concatenate([k_hist.astype(k.dtype), k], axis=1)
        v_all = jnp.concatenate([v_hist.astype(v.dtype), v], axis=1)
        o = cached_attention(q, k_all, v_all, attn_sinks)
    y_attn = o @ w_attn_o
    merged = jax.nn.sigmoid(g_conv) * y_conv + jax.nn.sigmoid(g_attn) * y_attn
    return merged @ w_mix_out, new_conv, k_all[:, -WINDOW:], v_all[:, -WINDOW:]

def swiglu(x, w_gate, w_up, w_down):
    return (jax.nn.silu(x @ w_gate) * (x @ w_up)) @ w_down

def route(h, w_router, router_bias):
    n = h.shape[0]
    scores = jax.nn.sigmoid(jnp.matmul(h, w_router, preferred_element_type=jnp.float32))
    biased = scores + router_bias.astype(jnp.float32)
    grouped = biased.reshape(n, N_EXPERT_GROUPS, N_EXPERTS // N_EXPERT_GROUPS)
    group_score = jnp.sum(lax.top_k(grouped, 2)[0], axis=-1)
    _, top_groups = lax.top_k(group_score, TOPK_GROUPS)
    group_mask = jnp.sum(jax.nn.one_hot(top_groups, N_EXPERT_GROUPS, dtype=jnp.float32), axis=-2) > 0
    expert_mask = jnp.repeat(group_mask, N_EXPERTS // N_EXPERT_GROUPS, axis=-1)
    _, top_idx = lax.top_k(jnp.where(expert_mask, biased, -jnp.inf), TOP_K)
    top_s = jnp.take_along_axis(scores, top_idx, axis=-1)
    top_w = top_s / jnp.sum(top_s, axis=-1, keepdims=True) * ROUTED_SCALE
    return top_idx.astype(jnp.int32), top_w

def routed_experts(h, top_idx, top_w, w_gate, w_up, w_down):
    n, d = h.shape
    a = n * TOP_K
    n_blocks = -(-a // DISPATCH_BLOCK) + N_EXPERTS
    flat_e = top_idx.reshape(a)
    order = jnp.argsort(flat_e).astype(jnp.int32)
    e_sorted = flat_e[order]
    counts = jnp.zeros((N_EXPERTS,), jnp.int32).at[flat_e].add(1)
    padded = (counts + DISPATCH_BLOCK - 1) // DISPATCH_BLOCK * DISPATCH_BLOCK
    pad_end = jnp.cumsum(padded)
    pad_start = pad_end - padded
    start = jnp.cumsum(counts) - counts
    dest = pad_start[e_sorted] + jnp.arange(a, dtype=jnp.int32) - start[e_sorted]
    slot = jnp.full((n_blocks * DISPATCH_BLOCK,), a, jnp.int32).at[dest].set(order)
    tok = jnp.append(jnp.arange(a, dtype=jnp.int32) // TOP_K, n)[slot]
    wt = jnp.append(top_w.reshape(a), 0.0)[slot]
    block_e = jnp.minimum(jnp.searchsorted(pad_end, jnp.arange(n_blocks) * DISPATCH_BLOCK, side='right'), N_EXPERTS - 1)
    h_pad = jnp.concatenate([h, jnp.zeros((1, d), h.dtype)], axis=0)

    def expert_block(args):
        e, tok_b, wt_b = args
        xb = h_pad[tok_b]
        return swiglu(xb, w_gate[e], w_up[e], w_down[e]) * wt_b[:, None].astype(h.dtype)

    yb = lax.map(expert_block, (block_e, tok.reshape(n_blocks, DISPATCH_BLOCK), wt.reshape(n_blocks, DISPATCH_BLOCK)))
    return jnp.zeros((n + 1, d), h.dtype).at[tok].add(yb.reshape(-1, d))[:n]

def layer(x, c, pos, conv_hist, k_hist, v_hist, w_ada, b_ada, w_in, w_conv, w_conv_out, w_attn_o,
          attn_sinks, w_mix_out, w_router, router_bias, w_exp_gate, w_exp_up, w_exp_down,
          w_sh_gate, w_sh_up, w_sh_down):
    mod = jax.nn.silu(c) @ w_ada + b_ada
    sh1, sc1, g1, sh2, sc2, g2 = jnp.split(mod[:, None, :], 6, axis=-1)
    h = rms_norm(x) * (1 + sc1) + sh1
    mix, new_conv, new_k, new_v = token_mixer(h, pos, conv_hist, k_hist, v_hist, w_in, w_conv,
                                              w_conv_out, w_attn_o, attn_sinks, w_mix_out)
    x = x + g1 * mix
    h = rms_norm(x) * (1 + sc2) + sh2
    b, t, d = h.shape
    hf = h.reshape(b * t, d)
    top_idx, top_w = route(hf, w_router, router_bias)
    ffn = swiglu(hf, w_sh_gate, w_sh_up, w_sh_down) + routed_experts(hf, top_idx, top_w, w_exp_gate, w_exp_up, w_exp_down)
    x = x + g2 * ffn.reshape(b, t, d)
    return x, new_conv, new_k, new_v

def setup_inputs(seed: int = 0) -> dict:
    key = jax.random.key(seed)
    ks = jax.random.split(key, 24)

    def nrm(k, shape, s):
        return jax.random.normal(k, shape, jnp.float32) * s

    L = DEPTH
    return {
        'x_prompt': nrm(ks[0], (BATCH, SEQ, D_MODEL), 1.0),
        'x_sample': nrm(ks[1], (DEC_BATCH, DEC_SEQ, D_MODEL), 1.0),
        'cache_k': nrm(ks[2], (L, DEC_BATCH, WINDOW, N_KV_HEADS, HEAD_DIM), 1.0),
        'cache_v': nrm(ks[3], (L, DEC_BATCH, WINDOW, N_KV_HEADS, HEAD_DIM), 1.0),
        'state_conv': nrm(ks[4], (L, DEC_BATCH, CONV_W - 1, D_CONV), 1.0),
        'c_prompt': nrm(ks[5], (BATCH, D_MODEL), 1.0),
        'c_sample': nrm(ks[6], (DEC_BATCH, D_MODEL), 1.0),
        'w_ada': nrm(ks[7], (L, D_MODEL, 6 * D_MODEL), 0.5 * D_MODEL ** -0.5),
        'b_ada': nrm(ks[8], (L, 6 * D_MODEL), 0.02),
        'w_in': nrm(ks[9], (L, D_MODEL, D_IN), D_MODEL ** -0.5),
        'w_conv': nrm(ks[10], (L, CONV_W, D_CONV), CONV_W ** -0.5),
        'w_conv_out': nrm(ks[11], (L, D_CONV, D_MODEL), D_CONV ** -0.5),
        'w_attn_o': nrm(ks[12], (L, Q_DIM, D_MODEL), Q_DIM ** -0.5),
        'attn_sinks': nrm(ks[13], (L, N_HEADS), 0.5),
        'w_mix_out': nrm(ks[14], (L, D_MODEL, D_MODEL), D_MODEL ** -0.5),
        'w_router': nrm(ks[15], (L, D_MODEL, N_EXPERTS), D_MODEL ** -0.5),
        'router_bias': nrm(ks[16], (L, N_EXPERTS), 0.01),
        'w_exp_gate': nrm(ks[17], (L, N_EXPERTS, D_MODEL, D_EXPERT), D_MODEL ** -0.5),
        'w_exp_up': nrm(ks[18], (L, N_EXPERTS, D_MODEL, D_EXPERT), D_MODEL ** -0.5),
        'w_exp_down': nrm(ks[19], (L, N_EXPERTS, D_EXPERT, D_MODEL), D_EXPERT ** -0.5),
        'w_sh_gate': nrm(ks[20], (L, D_MODEL, D_SHARED), D_MODEL ** -0.5),
        'w_sh_up': nrm(ks[21], (L, D_MODEL, D_SHARED), D_MODEL ** -0.5),
        'w_sh_down': nrm(ks[22], (L, D_SHARED, D_MODEL), D_SHARED ** -0.5),
        'final_gain': 1.0 + nrm(ks[23], (D_MODEL,), 0.02),
    }

def reference(x_prompt, x_sample, cache_k, cache_v, state_conv, c_prompt, c_sample,
              w_ada, b_ada, w_in, w_conv, w_conv_out, w_attn_o, attn_sinks, w_mix_out,
              w_router, router_bias, w_exp_gate, w_exp_up, w_exp_down,
              w_sh_gate, w_sh_up, w_sh_down, final_gain):
    pos_p = jnp.arange(x_prompt.shape[1], dtype=jnp.int32)
    pos_s = PAST_LEN + jnp.arange(x_sample.shape[1], dtype=jnp.int32)
    yp, ys = x_prompt, x_sample
    p_conv, p_k, p_v, s_conv, s_k, s_v = [], [], [], [], [], []
    for l in range(DEPTH):
        weights = (w_ada[l], b_ada[l], w_in[l], w_conv[l], w_conv_out[l], w_attn_o[l], attn_sinks[l],
                   w_mix_out[l], w_router[l], router_bias[l], w_exp_gate[l], w_exp_up[l], w_exp_down[l],
                   w_sh_gate[l], w_sh_up[l], w_sh_down[l])
        yp, pc, pk, pv = layer(yp, c_prompt, pos_p, None, None, None, *weights)
        ys, sc, sk, sv = layer(ys, c_sample, pos_s, state_conv[l], cache_k[l], cache_v[l], *weights)
        p_conv.append(pc)
        p_k.append(pk)
        p_v.append(pv)
        s_conv.append(sc)
        s_k.append(sk)
        s_v.append(sv)
    y_prompt = rms_norm(yp) * final_gain
    y_sample = rms_norm(ys) * final_gain
    return (y_prompt, y_sample, jnp.stack(p_conv), jnp.stack(p_k), jnp.stack(p_v),
            jnp.stack(s_conv), jnp.stack(s_k), jnp.stack(s_v))


_drawn_inputs = setup_inputs


def setup_inputs(seed=0):
    import zlib

    import numpy as np

    out = dict(_drawn_inputs(seed))
    spreads = {}
    factors = {'attn_sinks': 8.0, 'final_gain': 2.904}
    for name, (base, spread) in spreads.items():
        noise = np.random.default_rng([zlib.crc32(name.encode()), seed]).standard_normal(out[name].shape)
        drawn = base * np.exp(spread * noise) if base else spread * noise
        out[name] = __import__('jax').numpy.asarray(drawn.astype(out[name].dtype))
    for name, factor in factors.items():
        out[name] = (out[name] * factor).astype(out[name].dtype)
    return out
```

```python
import numpy as np
import concourse.bass as bass
from concourse import mybir
from contextlib import ExitStack

F32 = mybir.dt.float32
F32R = mybir.dt.float32r
BF16 = mybir.dt.bfloat16
I32 = mybir.dt.int32
ALU = mybir.AluOpType
ACT = mybir.ActivationFunctionType
AX = mybir.AxisListType

P = 128
D = 1024
KT = D // P
SEQ = 1024
DEC = 64
TOK = SEQ + DEC
NT = -(-TOK // P)
PAST = 512
CHUNK = 64
WINDOW = 128
NQ, NKV, HD = 16, 4, 64
HALF = HD // 2
SCALE = HD ** -0.5
NE, TOPK, NG, GS, TOPG = 64, 8, 8, 8, 4
DE = 256
DSH = 256
ROUTED_SCALE = 2.5
EPS = 1e-6
KVD = NKV * HD
C_B, C_C, C_X, C_Q, C_K, C_V, C_GC, C_GA = 0, 1024, 2048, 3072, 4096, 4352, 4608, 5632
D_IN = 6656
NCH, CH = 4, TOK // 4
BLK = P
MAX_BLOCKS = NE + (TOK * TOPK - NE) // BLK
NBP = MAX_BLOCKS + 5
NCOL = NBP
NTHR = -(-TOK // BLK)
KEY0 = 32768.0
NOWHERE = float(1 << 20)
SH1, SC1, G1, SH2, SC2, G2 = range(6)

C_ID = 0
C_TRI = C_ID + P
C_IP = C_TRI + P
C_IC = C_IP + P
C_VAL = C_IC + NCOL
C_THR = C_VAL + NT * TOPK
C_IB = C_THR + NTHR
C_LOW = C_IB + NBP
C_ROW = C_LOW + NG * NG
C_COS = C_ROW + 1
C_SIN = C_COS + NT * HALF
C_END = C_SIN + NT * HALF


def constants():
    c = np.zeros((P, C_END), np.float32)
    r = np.arange(P)
    c[:, C_ID:C_ID + P] = np.eye(P)
    c[:, C_TRI:C_TRI + P] = r[:, None] < r[None, :]
    c[:, C_IP:C_IP + P] = r[None, :]
    c[:, C_IC:C_IC + NCOL] = np.arange(NCOL)[None, :]
    t = np.arange(NT)[:, None] * P
    val = t[None] + r[:, None, None] + 1 + np.zeros((1, 1, TOPK))
    c[:, C_VAL:C_VAL + NT * TOPK] = val.reshape(P, -1)
    c[:, C_THR:C_THR + NTHR] = np.arange(NTHR)[None] * BLK
    c[:, C_IB:C_IB + NBP] = np.arange(NBP)[None]
    c[:, C_ROW] = r
    g = np.arange(NG)
    c[:, C_LOW:C_LOW + NG * NG] = (g[None, :] < g[:, None]).reshape(1, -1)
    pos = np.concatenate([np.arange(SEQ), PAST + np.arange(NT * P - SEQ)]).astype(np.float32)
    freq = (10000.0 ** (-np.arange(HALF) / HALF)).astype(np.float32)
    ang = (pos[:, None] * freq[None, :]).astype(np.float32).astype(np.float64)
    for at, f in ((C_COS, np.cos), (C_SIN, np.sin)):
        c[:, at:at + NT * HALF] = f(ang).reshape(NT, P, HALF).transpose(1, 0, 2).reshape(P, -1)
    return c


class Link:

    def __init__(self, eng, sem):
        self.eng, self.sem, self.n = eng, sem, 0

    def __call__(self, ins):
        self.n += 1
        ins.then_inc(self.sem, 1)
        self.eng.wait_ge(self.sem, self.n)


def rows_of(t):
    return P if t < NT - 1 else TOK - (NT - 1) * P


class Program:
    def __init__(self, nc, I, O):
        self.nc, self.I, self.O = nc, I, O
        self.top = ExitStack()
        self.links = {}

    def link_of(self, eng, name):
        if name not in self.links:
            self.links[name] = Link(eng, self.sem(f"chain_{name}"))
        self.links[name].eng = eng
        return self.links[name]

    def sem(self, name):
        return self.top.enter_context(self.nc.semaphore(name))

    def sb(self, name, shape, dt=F32):
        cm = self.nc.sbuf_tensor(name, shape, dt)
        t = cm.__enter__()
        self.live[name] = cm
        return t

    def free(self, *names):
        for n in names:
            self.live.pop(n).__exit__(None, None, None)

    def build(self):
        nc = self.nc
        self.live = {}
        with self.top:
            self.con = self.sb("con", [P, C_END])
            self.ident = self.con[:, C_ID:C_ID + P]
            self.modcol = self.sb("modcol", [P, 2, 16])
            self.mod_rows = nc.dram_tensor("mod_rows", (96, P), F32, kind="Internal").ap()
            self.h2_rows = nc.dram_tensor("h2_rows", (TOK, D), F32, kind="Internal").ap()
            self.sum_rows = nc.dram_tensor("sum_rows", (TOK, D), F32, kind="Internal").ap()
            self.sum_cleared = self.sem("sum_cleared")
            self.loaded_con = self.sem("loaded_con")
            self.stored = self.sem("stored")
            self.n_stored = 0
            self.score = self.sb("score", [P, NT, NE])
            self.place_w = self.sb("place_w", [P, NCOL])
            self.place_x = self.sb("place_x", [P, NCOL], I32)
            self.blk_ord = self.sb("blk_ord", [1, NBP], I32)
            self.blk_split = self.sb("blk_split", [1, NBP], I32)
            self.ord_e = self.sb("ord_e", [1, NE], I32)
            self.n_blocks = self.sb("n_blocks", [1, 1], I32)
            self.n_used = self.sb("n_used", [1, 1], I32)
            early_late = self.sb("early_late", [P, NT * D])
            self.wqkv = early_late[:, 0:2 * KT * 512].rearrange("p (b k n) -> p b k n", b=2, k=KT)
            self.oT = early_late[:, 0:KT * TOK].rearrange("p (k n) -> p k n", k=KT)
            self.x2 = early_late[:, :].rearrange("p (t n) -> p t n", t=NT)
            self.hT = self.sb("hT", [P, KT, TOK])
            self.h2T = self.hT
            self.ada_norm1()
            self.qT = self.sb("qT", [HD, 17, NQ, CHUNK])
            self.kT = self.sb("kT", [HD, NKV, SEQ + WINDOW + DEC])
            self.V2 = self.sb("V2", [P, 19, KVD])
            self.qkv()
            self.attention()
            self.free("V2", "kT", "qT")
            self.mT = self.sb("mT", [P, KT, TOK])
            self.cT = self.sb("cT_all", [P, KT, TOK])
            self.conv_branch()
            self.merge()
            self.free("cT_all")
            self.mix()
            self.free("mT")
            self.routing()
            self.shared()
            self.free("hT")
            self.experts()
            self.combine()

    def x_rows(self, t):
        return self.I["x_prompt"][0, t * P:(t + 1) * P, :] if t < NT - 1 else self.I["x_sample"][0]

    def ada_norm1(self):
        nc, I = self.nc, self.I
        S = self.sem
        c_loaded, b_loaded = S("c_loaded"), S("b_ada_loaded")
        w_loaded = [S("w_ada_loaded0"), S("w_ada_loaded1")]
        c_sig, c_silu, chunk_done, row_done, mod_t, mod_col, mod_stored = map(
            S, ("c_sig", "c_silu", "ada_chunk", "ada_row", "mod_t", "mod_col", "mod_stored"))
        x_loaded = [S(f"x_loaded{i}") for i in range(3)]
        sq, ms, rt, xn_ready, xt, ev_a, ev_v = map(S, ("n1_sq", "n1_ms", "n1_root", "n1_xn", "n1_xt", "n1_ev_act", "n1_ev_dve"))
        self.wq_loaded = [S("wq_loaded0"), S("wq_loaded1")]
        w_ada = I["w_ada"][0]
        NC = 12
        FIRST = 4
        hT, mod = self.hT, self.modcol
        with ExitStack() as st:
            sb = lambda n, s, d=F32: st.enter_context(nc.sbuf_tensor(n, s, d))
            ps = lambda n, s, d=F32: st.enter_context(nc.psum_tensor(n, s, d))
            wbuf = sb("w_ada_buf", [P, 2, KT, 1024])
            c_ld = sb("c_ld", [P, 2, KT])
            c_sg = sb("c_sg", [P, 2, KT])
            cT = sb("cT", [P, KT, 2])
            mrow = sb("mrow", [2, NC, 512])
            x = sb("n1_x", [P, 3, D])
            xn = sb("n1_xn_b", [P, 2, D])
            junk = sb("n1_junk", [P, D])
            ss, m, r, ri = (sb(f"n1_{n}", [P, NT]) for n in ("ss", "m", "r", "ri"))
            pm = [ps(f"pm{i}", [2, 512]) for i in range(2)]
            pcol = ps("pcol", [P, 512])[:, 0:32].rearrange("p (j g) -> p j g", g=2)
            pt = [ps(f"n1_pt{i}", [P, 2, 512]) for i in range(2)]
            with nc.Block() as block:
                @block.sync
                def _(sp):
                    for v in range(6):
                        if v >= 2:
                            sp.wait_ge(chunk_done, 2 * v - 2)
                        sp.dma_start(wbuf[:, v % 2], w_ada[:, v * 1024:(v + 1) * 1024]
                                     .rearrange("(p k) n -> p k n", k=KT)).then_inc(w_loaded[v % 2], 16)
                    for cb in range(2):
                        sp.dma_start(self.wqkv[:, cb], I["w_in"][0][:, C_Q + cb * 512:C_Q + (cb + 1) * 512]
                                     .rearrange("(k p) n -> p k n", p=P)).then_inc(self.wq_loaded[cb], 16)
                    sp.wait_ge(row_done, NC)
                    sp.dma_start(self.mod_rows.rearrange("(g j) p -> g (j p)", g=2), mrow[:, :, :].rearrange("g c n -> g (c n)")).then_inc(mod_stored, 16)
                    sp.wait_ge(mod_stored, 16)

                @block.gpsimd
                def _(pool):
                    for t in range(NT):
                        R = rows_of(t)
                        if t >= 3:
                            pool.wait_ge(xn_ready, t - 2)
                        pool.dma_start(x[:R, t % 3, :], self.x_rows(t)).then_inc(x_loaded[t % 3], 16)

                @block.scalar
                def _(act):
                    act.dma_start(c_ld[:, 0, :], I["c_prompt"][0].rearrange("(p k) -> p k", k=KT)).then_inc(c_loaded, 16)
                    act.dma_start(c_ld[:, 1, :], I["c_sample"][0].rearrange("(p k) -> p k", k=KT)).then_inc(c_loaded, 16)
                    act.dma_start(mrow[:, :, :].rearrange("g c n -> g (c n)"), I["b_ada"][0].partition_broadcast(2)).then_inc(b_loaded, 16)
                    act.dma_start(self.con[:, :], I["con"]).then_inc(self.loaded_con, 16)
                    link = self.link_of(act, "act")
                    act.wait_ge(c_loaded, 32)
                    act.activation(c_sg[:, :, :], c_ld[:, :, :], ACT.Sigmoid).then_inc(c_sig, 1)

                    def norm(t):
                        R = rows_of(t)
                        act.wait_ge(x_loaded[t % 3], 16 * (t // 3 + 1))
                        link(act.activation(junk[:R, :], x[:R, t % 3, :], ACT.Square, accum_out=ss[:R, t:t + 1]))
                        act.sem_inc(sq, 1)
                        act.wait_ge(ms, t + 1)
                        act.activation(r[:R, t:t + 1], m[:R, t:t + 1], ACT.Sqrt).then_inc(rt, 1)

                    def evac(t):
                        g = int(t == NT - 1)
                        R = rows_of(t)
                        act.wait_ge(xt, t + 1)
                        for k in range(4):
                            last = act.activation(hT[:, k, t * P:t * P + R], pt[t % 2][:, 0, k * P:k * P + R],
                                                  ACT.Identity, bias=mod[:, g, 8 * SH1 + k:8 * SH1 + k + 1],
                                                  scale=mod[:, g, 8 * SC1 + k:8 * SC1 + k + 1])
                        last.then_inc(ev_a, 1)

                    norm(0)
                    norm(1)
                    act.wait_ge(mod_col, 1)
                    for t in range(NT):
                        evac(t)
                        if t + 2 < NT:
                            norm(t + 2)

                @block.vector
                def _(dve):
                    link = self.link_of(dve, "dve")

                    def norm(t):
                        R = rows_of(t)
                        dve.wait_ge(sq, t + 1)
                        dve.tensor_scalar(m[:R, t:t + 1], ss[:R, t:t + 1], 1.0 / D, EPS, ALU.mult, ALU.add).then_inc(ms, 1)
                        dve.wait_ge(rt, t + 1)
                        link(dve.reciprocal(ri[:R, t:t + 1], r[:R, t:t + 1]))
                        if t >= 2:
                            dve.wait_ge(xt, t - 1)
                        dve.tensor_scalar(xn[:R, t % 2, :], x[:R, t % 3, :], ri[:R, t:t + 1], None,
                                          ALU.mult).then_inc(xn_ready, 1)

                    def row(c):
                        dve.wait_ge(chunk_done, c + 1)
                        dve.scalar_tensor_tensor(mrow[:, c, :], pm[c % 2][:, :], 1.0 if c // 2 in (SC1, SC2) else 0.0,
                                                 mrow[:, c, :], ALU.add, ALU.add).then_inc(row_done, 1)

                    def evac(t):
                        g = int(t == NT - 1)
                        R = rows_of(t)
                        dve.wait_ge(xt, t + 1)
                        for k in range(4, 8):
                            last = dve.tensor_scalar(hT[:, k, t * P:t * P + R], pt[t % 2][:, 1, (k - 4) * P:(k - 4) * P + R],
                                                     mod[:, g, 8 * SC1 + k:8 * SC1 + k + 1],
                                                     mod[:, g, 8 * SH1 + k:8 * SH1 + k + 1], ALU.mult, ALU.add)
                        last.then_inc(ev_v, 1)

                    dve.wait_ge(c_sig, 1)
                    dve.tensor_tensor(cT[:, :, :].rearrange("p k g -> p g k"), c_ld[:, :, :], c_sg[:, :, :],
                                      ALU.mult).then_inc(c_silu, 1)
                    norm(0)
                    norm(1)
                    dve.wait_ge(b_loaded, 16)
                    for c in range(FIRST):
                        row(c)
                    dve.wait_ge(mod_t, 1)
                    link(dve.tensor_copy(mod[:, :, :], pcol[:, :, :].rearrange("p j g -> p g j")))
                    dve.sem_inc(mod_col, 1)
                    for t in range(NT):
                        evac(t)
                        if t + 2 < NT:
                            norm(t + 2)
                        if FIRST + t < NC:
                            row(FIRST + t)

                @block.tensor
                def _(pe):
                    def chunk(c):
                        if c % 2 == 0:
                            pe.wait_ge(w_loaded[c // 2 % 2], 16 * (c // 4 + 1))
                        if c >= 2:
                            pe.wait_ge(row_done, c - 1)
                        for k in range(KT):
                            last = pe.matmul(pm[c % 2][:, :], cT[:, k, :], wbuf[:, c // 2 % 2, k, c % 2 * 512:(c % 2 + 1) * 512],
                                             start=(k == 0), stop=(k == KT - 1))
                        last.then_inc(chunk_done, 1)

                    def tile(t):
                        R = rows_of(t)
                        pe.wait_ge(xn_ready, t + 1)
                        if t >= 2:
                            pe.wait_ge(ev_a, t - 1)
                            pe.wait_ge(ev_v, t - 1)
                        for k in range(KT):
                            last = pe.transpose(pt[t % 2][:, k // 4, (k % 4) * P:(k % 4) * P + R],
                                                xn[:R, t % 2, k * P:(k + 1) * P], self.ident[:R, :R])
                        last.then_inc(xt, 1)

                    pe.wait_ge(self.loaded_con, 16)
                    pe.wait_ge(c_silu, 1)
                    for c in range(FIRST):
                        chunk(c)
                    pe.wait_ge(row_done, FIRST)
                    for j in range(16):
                        last = pe.transpose(pcol[:, j, :], mrow[:, j // 4, j % 4 * P:(j % 4 + 1) * P], self.ident[0:2, 0:2])
                    last.then_inc(mod_t, 1)
                    for t in range(NT):
                        tile(t)
                        if FIRST + t < NC:
                            chunk(FIRST + t)

    def qkv(self):
        nc, I = self.nc, self.I
        S = self.sem
        w_loaded = self.wq_loaded
        proj, rot_done, roped, q_t, q_ev, v_ev, kc, kst, vst = map(
            S, ("qkv_proj", "qkv_read", "qkv_roped", "qkv_t", "qkv_ev", "qkv_v_ev", "kcache", "k_tail", "v_tail"))
        w_in = I["w_in"][0]
        kT, qT, V2, hT = self.kT, self.qT, self.V2, self.hT
        cos = self.con[:, C_COS:C_COS + NT * HALF].rearrange("p (t h) -> p t h", h=HALF)
        sin = self.con[:, C_SIN:C_SIN + NT * HALF].rearrange("p (t h) -> p t h", h=HALF)
        with ExitStack() as st:
            sb = lambda n, s, d=F32: st.enter_context(nc.sbuf_tensor(n, s, d))
            ps = lambda n, s, d=F32: st.enter_context(nc.psum_tensor(n, s, d))
            w = self.wqkv
            rot = sb("rot", [P, 2, 512])
            tsin = sb("tsin", [P, 512])
            kc_ld = sb("kc_ld", [P, KVD])
            kkeep = sb("kkeep", [P, 2, KVD])
            vkeep = sb("vkeep", [P, 2, KVD])
            pp = [ps(f"qk_pp{i}", [P, 512]) for i in range(2)]
            pt = [ps(f"qk_pt{i}", [HD, 8, P]) for i in range(2)]
            units = [(cb, t) for cb in range(3) for t in range(NT)]
            NU = len(units)
            with nc.Block() as block:
                @block.sync
                def _(sp):
                    sp.wait_ge(proj, NT)
                    sp.dma_start(w[:, 0], w_in[:, C_Q + 2 * 512:C_Q + 3 * 512]
                                 .rearrange("(k p) n -> p k n", p=P)).then_inc(w_loaded[0], 16)
                    sp.dma_start(kc_ld[:, :], I["cache_k"][0, 0].rearrange("w h d -> w (h d)")).then_inc(kc, 16)
                    sp.dma_start(V2[:, 16, :], I["cache_v"][0, 0].rearrange("w h d -> w (h d)")).then_inc(kc, 16)
                    O = self.O
                    keep = WINDOW - DEC
                    for o, c in (("sample_k", "cache_k"), ("sample_v", "cache_v")):
                        sp.dma_start(O[o][0, 0, 0:keep].rearrange("w h d -> w (h d)"),
                                     I[c][0, 0, DEC:WINDOW].rearrange("w h d -> w (h d)")).then_inc(self.stored, 16)
                    sp.wait_ge(kst, 2)
                    sp.wait_ge(vst, 2)
                    for g, (ok, ov) in enumerate((("prompt_k", "prompt_v"), ("sample_k", "sample_v"))):
                        a, b = (0, P) if g == 0 else (keep, WINDOW)
                        sp.dma_start(O[ok][0, 0, a:b].rearrange("w h d -> w (h d)"), kkeep[0:b - a, g, :]).then_inc(self.stored, 16)
                        sp.dma_start(O[ov][0, 0, a:b].rearrange("w h d -> w (h d)"), vkeep[0:b - a, g, :]).then_inc(self.stored, 16)
                    self.n_stored += 6
                    sp.wait_ge(self.stored, 16 * self.n_stored)
                    sp.wait_ge(kc, 32)

                @block.tensor
                def _(pe):
                    def transposes(u):
                        cb, t = units[u]
                        R = rows_of(t)
                        pe.wait_ge(roped, u + 1)
                        if u >= 2:
                            pe.wait_ge(q_ev, u - 1)
                        for h in range(8 if cb < 2 else 4):
                            last = pe.transpose(pt[u % 2][:, h, 0:R], rot[:R, u % 2, h * HD:(h + 1) * HD],
                                                self.ident[:R, :R])
                        last.then_inc(q_t, 1)

                    for u, (cb, t) in enumerate(units):
                        R = rows_of(t)
                        if t == 0:
                            pe.wait_ge(w_loaded[cb % 2], 16 * (cb // 2 + 1))
                        if u >= 2:
                            pe.wait_ge(rot_done, u - 1)
                            if units[u - 2][0] == 2:
                                pe.wait_ge(v_ev, u - 2 - 2 * NT + 1)
                        for k in range(KT):
                            last = pe.matmul(pp[u % 2][:R, :], hT[:, k, t * P:t * P + R], w[:, cb % 2, k, :],
                                             start=(k == 0), stop=(k == KT - 1))
                        last.then_inc(proj, 1)
                        if u:
                            transposes(u - 1)
                    transposes(NU - 1)
                    pe.wait_ge(kc, 32)
                    pe.wait_ge(q_ev, NU - 1)
                    for h in range(NKV):
                        last = pe.transpose(pt[NU % 2][:, h, :], kc_ld[:, h * HD:(h + 1) * HD], self.ident)
                    last.then_inc(q_t, 1)

                @block.vector
                def _(dve):
                    link = self.link_of(dve, "dve")
                    for u, (cb, t) in enumerate(units):
                        R = rows_of(t)
                        nh = 8 if cb < 2 else 4
                        dve.wait_ge(proj, u + 1)
                        if u >= 2:
                            dve.wait_ge(q_t, u - 1)
                        src = pp[u % 2][:R, 0:nh * HD].rearrange("p (h s d) -> p h s d", s=2, d=HALF)
                        ts = tsin[:R, 0:nh * HD].rearrange("p (h s d) -> p h s d", s=2, d=HALF)
                        dst = rot[:R, u % 2, 0:nh * HD].rearrange("p (h s d) -> p h s d", s=2, d=HALF)
                        c = cos[:R, t, :].unsqueeze(1).to_broadcast([R, nh, HALF])
                        s = sin[:R, t, :].unsqueeze(1).to_broadcast([R, nh, HALF])
                        for half in range(2):
                            dve.tensor_tensor(dst[:, :, half, :], src[:, :, half, :], c, ALU.mult)
                            last = dve.tensor_tensor(ts[:, :, half, :], src[:, :, 1 - half, :], s, ALU.mult)
                        link(last)
                        dve.sem_inc(rot_done, 1)
                        dve.tensor_tensor(dst[:, :, 0, :], dst[:, :, 0, :], ts[:, :, 0, :], ALU.subtract)
                        link(dve.tensor_tensor(dst[:, :, 1, :], dst[:, :, 1, :], ts[:, :, 1, :], ALU.add))
                        dve.sem_inc(roped, 1)
                        if cb == 2 and t >= NT - 2:
                            dve.tensor_copy(kkeep[:R, t - NT + 2, :], rot[:R, u % 2, 0:KVD]).then_inc(kst, 1)

                @block.scalar
                def _(act):
                    for u, (cb, t) in enumerate(units):
                        R = rows_of(t)
                        nch = R // CHUNK
                        if cb == 2:
                            act.wait_ge(rot_done, u + 1)
                            v = pp[u % 2][:R, KVD:2 * KVD]
                            if t >= NT - 2:
                                act.copy(vkeep[:R, t - NT + 2, :], v).then_inc(vst, 1)
                            if t < NT - 1:
                                act.copy(V2[:, 2 * t, :], v)
                                if t:
                                    act.copy(V2[CHUNK:P, 2 * t - 1, :], v[0:CHUNK])
                                last = act.copy(V2[0:CHUNK, 2 * t + 1, :], v[CHUNK:P])
                            else:
                                last = act.copy(V2[0:CHUNK, 18, :], v)
                            last.then_inc(v_ev, 1)
                        act.wait_ge(q_t, u + 1)
                        if cb < 2:
                            for c in range(nch):
                                last = act.copy(qT[:, 2 * t + c, cb * 8:cb * 8 + 8, :], pt[u % 2][:, :, c * CHUNK:(c + 1) * CHUNK])
                        else:
                            at = t * P if t < NT - 1 else SEQ + WINDOW
                            last = act.copy(kT[:, :, at:at + R], pt[u % 2][:, 0:NKV, 0:R])
                        last.then_inc(q_ev, 1)
                    act.wait_ge(q_t, NU + 1)
                    act.copy(kT[:, :, SEQ:SEQ + WINDOW], pt[NU % 2][:, 0:NKV, :]).then_inc(q_ev, 1)

    def attention(self):
        nc, I = self.nc, self.I
        S = self.sem
        sk, sc_done, mx, sexp, pn, t1d, t2d, ev1, ev2, od, oev, es_d = map(
            S, ("sink_loaded", "at_scores", "at_max", "at_exp", "at_probs", "at_t", "at_t_unused", "at_ev_act", "at_ev_dve",
                "at_o", "at_oev", "at_sinkdiff"))
        kT, qT, V2, oT = self.kT, self.qT, self.V2, self.oT
        units = [(n, hf) for n in range(17) for hf in range(2)]

        def keys(n):
            if n == 16:
                return SEQ, WINDOW, DEC, 16, 18
            if n == 0:
                return 0, CHUNK, 0, 0, None
            if n == 1:
                return 0, P, 0, 0, None
            return (n - 2) * CHUNK, P, CHUNK, n - 2, n

        with ExitStack() as st:
            sb = lambda n, s, d=F32: st.enter_context(nc.sbuf_tensor(n, s, d))
            ps = lambda n, s, d=F32: st.enter_context(nc.psum_tensor(n, s, d))
            sink = sb("sink", [P, 8])
            nsink = sb("nsink", [P, 8])
            m = sb("at_m", [P, 2, 4])
            nm = sb("at_nm", [P, 2, 4])
            ds_ = sb("at_ds", [P, 2, 4])
            es = sb("at_es", [P, 2, 4])
            rs = sb("at_rs", [P, 2, 4])
            z = sb("at_z", [P, 2, 4])
            rz = sb("at_rz", [P, 2, 4])
            pr = sb("at_p", [P, 2, 4, 192])
            pt1 = sb("at_pt1", [P, 2, 512])
            pt2 = sb("at_pt2", [CHUNK, 2, 512])
            sc = [ps(f"at_s{i}", [P, 2, 512]) for i in range(2)]
            p1 = ps("at_p1", [P, 512])
            p2 = ps("at_p2", [CHUNK, 512])
            po = [ps(f"at_po{i}", [CHUNK, 512]) for i in range(2)]
            with nc.Block() as block:
                @block.sync
                def _(sp):
                    for h in range(2):
                        src = I["attn_sinks"][0].rearrange("(j h) -> h j", h=2)[h:h + 1]
                        with nc.allow_non_contiguous_dma(reason="16 sinks"):
                            sp.dma_start(sink[h * CHUNK:(h + 1) * CHUNK, :], src.to_broadcast([CHUNK, 8])).then_inc(sk, 16)
                    sp.wait_ge(sk, 32)

                @block.tensor
                def _(pe):
                    def scores(u):
                        n, hf = units[u]
                        ks, a, b, _, _ = keys(n)
                        if u >= 2:
                            pe.wait_ge(sexp, u - 1)
                        for i in range(4):
                            j = hf * 4 + i
                            last = pe.matmul(sc[u % 2][:, i // 2, (i % 2) * 192:(i % 2) * 192 + a + b],
                                             qT[:, n, 2 * j:2 * j + 2, :], kT[:, j // 2, ks:ks + a + b],
                                             start=True, stop=True)
                        last.then_inc(sc_done, 1)

                    def transposes(u):
                        n, hf = units[u]
                        _, a, b, _, _ = keys(n)
                        pe.wait_ge(pn, u + 1)
                        if u:
                            pe.wait_ge(ev1, u)
                            pe.wait_ge(ev2, u)
                        for i in range(4):
                            last = pe.transpose(p1[0:a, i * P:(i + 1) * P], pr[:, u % 2, i, 0:a], self.ident)
                        if b:
                            for i in range(4):
                                last = pe.transpose(p2[:, i * P:(i + 1) * P], pr[:, u % 2, i, a:a + b], self.ident)
                        last.then_inc(t1d, 1)

                    def values(u):
                        n, hf = units[u]
                        _, a, b, va, vb = keys(n)
                        pe.wait_ge(ev1, u + 1)
                        pe.wait_ge(ev2, u + 1)
                        if u >= 2:
                            pe.wait_ge(oev, u - 1)
                        for i in range(2):
                            kv = (hf * 2 + i) * HD
                            last = pe.matmul(po[u % 2][:, i * 256:(i + 1) * 256], V2[0:a, va, kv:kv + HD],
                                             pt1[0:a, u % 2, i * 256:(i + 1) * 256], start=True, stop=(b == 0))
                            if b:
                                last = pe.matmul(po[u % 2][:, i * 256:(i + 1) * 256], V2[0:b, vb, kv:kv + HD],
                                                 pt2[0:b, u % 2, i * 256:(i + 1) * 256], start=False, stop=True)
                        last.then_inc(od, 1)

                    scores(0)
                    for u in range(len(units)):
                        if u + 1 < len(units):
                            scores(u + 1)
                        if u:
                            values(u - 1)
                        transposes(u)
                    values(len(units) - 1)

                @block.vector
                def _(dve):
                    link = self.link_of(dve, "dve")
                    dve.wait_ge(sk, 32)
                    link(dve.tensor_scalar(nsink[:, :], sink[:, :], -1.0, None, ALU.mult))

                    def head(u):
                        n, hf = units[u]
                        _, a, b, _, _ = keys(n)
                        b2 = u % 2
                        dve.wait_ge(sc_done, u + 1)
                        v = sc[b2][:, :, 0:384].rearrange("p b (a k) -> p b a k", a=2)[:, :, :, 0:a + b]
                        link(dve.tensor_reduce(m[:, b2, :].rearrange("p (b a) -> p b a", b=2), v, AX.X, ALU.max))
                        link(dve.scalar_tensor_tensor(nm[:, b2, :], m[:, b2, :], -SCALE, nsink[:, hf * 4:hf * 4 + 4], ALU.mult, ALU.min))
                        dve.tensor_tensor(ds_[:, b2, :], sink[:, hf * 4:hf * 4 + 4], nm[:, b2, :], ALU.add).then_inc(mx, 1)

                    def tail(u):
                        n, hf = units[u]
                        _, a, b, _, _ = keys(n)
                        b2 = u % 2
                        dve.wait_ge(sexp, u + 1)
                        link(dve.tensor_tensor(z[:, b2, :], rs[:, b2, :], es[:, b2, :], ALU.add))
                        link(dve.reciprocal(rz[:, b2, :], z[:, b2, :]))
                        dve.tensor_tensor(pr[:, b2, :, 0:a + b], pr[:, b2, :, 0:a + b],
                                          rz[:, b2, :].unsqueeze(2).to_broadcast([P, 4, a + b]), ALU.mult).then_inc(pn, 1)

                    def evac(u):
                        _, a, b, _, _ = keys(units[u][0])
                        dve.wait_ge(t1d, u + 1)
                        if u >= 2:
                            dve.wait_ge(od, u - 1)
                        if b:
                            dve.tensor_copy(pt2[:, u % 2, :], p2[:, :]).then_inc(ev2, 1)
                        else:
                            dve.sem_inc(ev2, 1)

                    head(0)
                    for u in range(len(units)):
                        if u + 1 < len(units):
                            head(u + 1)
                        tail(u)
                        evac(u)

                @block.scalar
                def _(act):
                    link = self.link_of(act, "act")

                    def exps(u):
                        n, hf = units[u]
                        _, a, b, _, _ = keys(n)
                        b2 = u % 2
                        act.wait_ge(mx, u + 1)
                        if u >= 2:
                            act.wait_ge(t1d, u - 1)
                        act.activation(es[:, b2, :], ds_[:, b2, :], ACT.Exp)
                        for i in range(4):
                            last = act.activation(pr[:, b2, i, 0:a + b], sc[b2][:, i // 2, (i % 2) * 192:(i % 2) * 192 + a + b],
                                                  ACT.Exp, bias=nm[:, b2, i:i + 1], scale=SCALE, accum_out=rs[:, b2, i:i + 1])
                        last.then_inc(sexp, 1)

                    def evac(u):
                        n, hf = units[u]
                        _, a, b, _, _ = keys(n)
                        act.wait_ge(t1d, u + 1)
                        if u >= 2:
                            act.wait_ge(od, u - 1)
                        act.copy(pt1[0:a, u % 2, :], p1[0:a, :]).then_inc(ev1, 1)

                    def out(u):
                        n, hf = units[u]
                        act.wait_ge(od, u + 1)
                        v = po[u % 2][:, :].rearrange("p (j h q) -> p h j q", h=2, q=CHUNK)
                        act.copy(oT[0:CHUNK, hf * 4:hf * 4 + 4, n * CHUNK:(n + 1) * CHUNK], v[:, 0])
                        act.copy(oT[CHUNK:P, hf * 4:hf * 4 + 4, n * CHUNK:(n + 1) * CHUNK], v[:, 1]).then_inc(oev, 1)

                    exps(0)
                    for u in range(len(units)):
                        if u + 1 < len(units):
                            exps(u + 1)
                        evac(u)
                        if u:
                            out(u - 1)
                    out(len(units) - 1)

    def conv_branch(self):
        nc, I, O = self.nc, self.I, self.O
        S = self.sem
        LEN = SEQ + DEC + 4
        w_in = I["w_in"][0]
        w_loaded = [S(f"cv_w{i}") for i in range(6)]
        small, job, c_read, x_read, b_read, st_t, st_ev, tail_ready, tail_t, tail_ev = map(
            S, ("cv_small", "cv_job", "cv_c_read", "cv_x_read", "cv_b_read", "cv_state_t", "cv_state_ev",
                "cv_tail_ready", "cv_tail_t", "cv_tail_ev"))
        cT, hT = self.cT, self.hT
        with ExitStack() as st:
            sb = lambda n, s, d=F32: st.enter_context(nc.sbuf_tensor(n, s, d))
            ps = lambda n, s, d=F32: st.enter_context(nc.psum_tensor(n, s, d))
            w = [sb(f"cv_wb{i}", [P, KT, P]) for i in range(6)]
            rows = sb("cv_rows", [40, P])
            wst = sb("cv_wst", [P, 40])
            cb = [sb(f"cv_c{i}", [P, TOK]) for i in range(2)]
            u = [sb(f"cv_u{i}", [P, LEN]) for i in range(2)]
            acc = sb("cv_acc", [P, LEN - 2])
            tail = sb("cv_tail", [P, 32])
            trow = sb("cv_trow", [32, P])
            ph = [ps(f"cv_ph{i}", [P, 4, 512]) for i in range(2)]
            COLS = (C_C, C_X, C_B)
            def pieces(half):
                p = ph[half]
                return ((0, p[:, 0:3, 0:CH], 0, 3 * CH), (3 * CH, p[:, 3, 0:SEQ - 3 * CH], 3 * CH, SEQ),
                        (SEQ + 2, p[:, 3, SEQ - 3 * CH:CH], SEQ, TOK))

            def cut(ap, n):
                return ap.rearrange("p (c n) -> p c n", n=CH) if n == 3 * CH else ap

            with nc.Block() as block:
                @block.sync
                def _(sp):
                    sp.dma_start(rows[0:24, :], I["w_conv"][0].rearrange("i (k p) -> (i k) p", p=P)).then_inc(small, 16)
                    sp.dma_start(rows[24:40, :], I["state_conv"][0, 0].rearrange("i (k p) -> (i k) p", p=P)).then_inc(small, 16)
                    for s in range(2):
                        for x in range(3):
                            sp.dma_start(w[3 * s + x][:, :, :], w_in[:, COLS[x] + s * P:COLS[x] + (s + 1) * P]
                                         .rearrange("(k p) n -> p k n", p=P)).then_inc(w_loaded[3 * s + x], 16)
                    with sp.Fori(0, KT // 2 - 1) as i:
                        for s in range(2):
                            for x in range(3):
                                sp.wait_ge(job, i * 6 + (3 * s + x + 1))
                                sp.dma_start(w[3 * s + x][:, :, :], w_in[:, bass.ds(i * 256 + (COLS[x] + 256 + s * P), P)]
                                             .rearrange("(k p) n -> p k n", p=P)).then_inc(w_loaded[3 * s + x], 16)
                    sp.wait_ge(tail_ev, 1)
                    for g, o in enumerate(("prompt_conv", "sample_conv")):
                        sp.dma_start(O[o][0, 0].rearrange("i (k p) -> (i k) p", p=P), trow[g * 16:(g + 1) * 16, :]).then_inc(self.stored, 16)
                    self.n_stored += 2
                    sp.wait_ge(self.stored, 16 * self.n_stored)

                @block.tensor
                def _(pe):
                    pe.wait_ge(small, 32)
                    pe.transpose(ph[0][:, 0, 0:40], rows[:, :], self.ident[0:40, 0:40]).then_inc(st_t, 1)
                    pe.wait_ge(st_ev, 1)
                    with pe.Fori(0, KT // 2) as i:
                        for s in range(2):
                            before = ((x_read, 0, 2), (b_read, 0, 2), (c_read, 1, 0)) if s == 0 else \
                                     ((x_read, 1, 2), (b_read, 1, 2), (c_read, 2, 0))
                            for x in range(3):
                                jj = 3 * s + x
                                sem, n, credit = before[x]
                                pe.wait_ge(sem, i * 2 + (n + credit))
                                pe.wait_ge(w_loaded[jj], i * 16 + 16)
                                for k in range(KT):
                                    for c in range(NCH):
                                        last = pe.matmul(ph[jj % 2][:, c, 0:CH], w[jj][:, k, :], hT[:, k, c * CH:(c + 1) * CH],
                                                         start=(k == 0), stop=(k == KT - 1))
                                last.then_inc(job, 1)
                    pe.wait_ge(tail_ready, 1)
                    pe.transpose(ph[0][0:32, 0, 0:P], tail[:, :], self.ident).then_inc(tail_t, 1)

                @block.scalar
                def _(act):
                    with act.Fori(0, KT // 2) as i:
                        for s in range(2):
                            act.wait_ge(job, i * 6 + (3 * s + 1))
                            act.wait_ge(x_read, i * 2 + (s + 1))
                            act.copy(cb[s][:, :].rearrange("p (c n) -> p c n", n=CH), ph[(3 * s) % 2][:, :, 0:CH]).then_inc(c_read, 1)
                    act.wait_ge(tail_t, 1)
                    act.copy(trow[:, :], ph[0][0:32, 0, 0:P]).then_inc(tail_ev, 1)

                @block.vector
                def _(dve):
                    own = S("cv_dve_link")
                    dve.sem_inc(x_read, 2)
                    dve.sem_inc(b_read, 2)
                    dve.wait_ge(st_t, 1)
                    dve.tensor_copy(wst[:, :], ph[0][:, 0, 0:40]).then_inc(st_ev, 1)
                    dve.wait_ge(st_ev, 1)
                    for s in range(2):
                        dve.memset(u[s][:, :], 0.0).then_inc(own, 1)
                    PER = 14
                    dve.wait_ge(own, 2)
                    with dve.Fori(0, KT // 2) as i:
                        count = [2]

                        def link(ins):
                            count[0] += 1
                            ins.then_inc(own, 1)
                            dve.wait_ge(own, i * PER + count[0])

                        for s in range(2):
                            m = i * 2 + s
                            link(dve.tensor_copy(u[s][:, SEQ + 2:SEQ + 4],
                                                 wst[:, 24:40].rearrange("p (j k) -> p j k", k=KT)[:, :, bass.ds(m, 1)].rearrange("p j k -> p (j k)")))
                            dve.wait_ge(job, i * 6 + (3 * s + 2))
                            dve.wait_ge(c_read, i * 2 + (s + 1))
                            for at, pv, a, b in pieces((3 * s + 1) % 2):
                                last = dve.tensor_tensor(cut(u[s][:, at + 2:at + 2 + b - a], b - a), cut(cb[s][:, a:b], b - a), pv, ALU.mult)
                            last.then_inc(x_read, 1)
                            dve.wait_ge(x_read, i * 2 + (s + 3))
                            n = LEN - 2
                            link(dve.tensor_scalar(acc[:, :], u[s][:, 0:n], wst[:, bass.ds(m, 1)], None, ALU.mult))
                            link(dve.scalar_tensor_tensor(acc[:, :], u[s][:, 1:1 + n], wst[:, bass.ds(m + 8, 1)], acc[:, :], ALU.mult, ALU.add))
                            link(dve.scalar_tensor_tensor(acc[:, :], u[s][:, 2:2 + n], wst[:, bass.ds(m + 16, 1)], acc[:, :], ALU.mult, ALU.add))
                            for g, at in enumerate((SEQ, SEQ + DEC + 2)):
                                link(dve.tensor_copy(tail[:, g * 16:g * 16 + 16].rearrange("p (j k) -> p j k", k=KT)[:, :, bass.ds(m, 1)].rearrange("p j k -> p (j k)"),
                                                u[s][:, at:at + 2]))
                            dve.wait_ge(job, i * 6 + (3 * s + 3))
                            for at, pv, a, b in pieces((3 * s + 2) % 2):
                                dst = cT[:, :, a:b][:, bass.ds(m, 1), :].rearrange("p k n -> p (k n)")
                                last = dve.tensor_tensor(cut(dst, b - a), cut(acc[:, at:at + b - a], b - a), pv, ALU.mult)
                            last.then_inc(b_read, 1)
                            dve.wait_ge(b_read, i * 2 + (s + 3))
                            link(dve.tensor_copy(acc[:, 0:2], u[s][:, 0:2]))
                        assert count[0] - 2 == PER, count
                    dve.engine_nop()
                    dve.sem_inc(tail_ready, 1)

    def merge(self):
        nc, I = self.nc, self.I
        S = self.sem
        w_loaded = [S(f"mg_w{i}") for i in range(4)]
        job, s1, s2, y1, y2, merged = map(S, ("mg_job", "mg_sig_conv", "mg_sig_attn", "mg_y_conv", "mg_y_attn", "mg_merged"))
        srcs = ((I["w_in"][0], C_GC), (I["w_conv_out"][0], 0), (I["w_in"][0], C_GA), (I["w_attn_o"][0], 0))
        hT, cT, oT = self.hT, self.cT, self.oT
        mT = self.mT
        with ExitStack() as st:
            sb = lambda n, s, d=F32: st.enter_context(nc.sbuf_tensor(n, s, d))
            ps = lambda n, s, d=F32: st.enter_context(nc.psum_tensor(n, s, d))
            w = [sb(f"mg_wb{i}", [P, KT, P]) for i in range(4)]
            t1 = sb("mg_t1", [P, NCH, CH])
            t2 = sb("mg_t2", [P, NCH, CH])
            ph = [ps(f"mg_ph{i}", [P, 4, 512]) for i in range(2)]
            moving = (hT, cT, hT, oT)
            with nc.Block() as block:
                @block.sync
                def _(sp):
                    for x, (src, at) in enumerate(srcs):
                        sp.dma_start(w[x][:, :, :], src[:, at:at + P].rearrange("(k p) n -> p k n", p=P)).then_inc(w_loaded[x], 16)
                    with sp.Fori(0, KT - 1) as i:
                        for x, (src, at) in enumerate(srcs):
                            sp.wait_ge(job, i * 4 + (x + 1))
                            sp.dma_start(w[x][:, :, :], src[:, bass.ds(i * P + (at + P), P)]
                                         .rearrange("(k p) n -> p k n", p=P)).then_inc(w_loaded[x], 16)

                @block.tensor
                def _(pe):
                    with pe.Fori(0, KT) as i:
                        before = ((s2, 1), (y2, 1), (s1, 1), (y1, 1))
                        for x in range(4):
                            pe.wait_ge(before[x][0], i + before[x][1])
                            pe.wait_ge(w_loaded[x], i * 16 + 16)
                            for k in range(KT):
                                for c in range(NCH):
                                    last = pe.matmul(ph[x % 2][:, c, 0:CH], w[x][:, k, :], moving[x][:, k, c * CH:(c + 1) * CH],
                                                     start=(k == 0), stop=(k == KT - 1))
                            last.then_inc(job, 1)

                @block.scalar
                def _(act):
                    act.sem_inc(s2, 1)
                    with act.Fori(0, KT) as i:
                        act.wait_ge(job, i * 4 + 1)
                        act.wait_ge(merged, i + 1)
                        act.activation(t1[:, :, :], ph[0][:, :, 0:CH], ACT.Sigmoid).then_inc(s1, 1)
                        act.wait_ge(job, i * 4 + 3)
                        act.activation(t2[:, :, :], ph[0][:, :, 0:CH], ACT.Sigmoid).then_inc(s2, 1)

                @block.vector
                def _(dve):
                    dve.sem_inc(merged, 1)
                    dve.sem_inc(y2, 1)
                    with dve.Fori(0, KT) as i:
                        dve.wait_ge(job, i * 4 + 2)
                        dve.wait_ge(s1, i + 1)
                        dve.tensor_tensor(t1[:, :, :], t1[:, :, :], ph[1][:, :, 0:CH], ALU.mult).then_inc(y1, 1)
                        dve.wait_ge(job, i * 4 + 4)
                        dve.wait_ge(s2, i + 2)
                        dve.tensor_tensor(t2[:, :, :], t2[:, :, :], ph[1][:, :, 0:CH], ALU.mult).then_inc(y2, 1)
                        dve.wait_ge(y1, i + 1)
                        dve.wait_ge(y2, i + 2)
                        dst = mT[:, bass.ds(i, 1), :].rearrange("p k (c n) -> p (k c) n", n=CH)
                        dve.tensor_tensor(dst, t1[:, :, :], t2[:, :, :], ALU.add).then_inc(merged, 1)

    def mix(self):
        nc, I = self.nc, self.I
        S = self.sem
        w_loaded, bc_loaded, mixed, x2_done, sq, ms, rt, h2_ready, h2_stored, t_done, t_ev, lg, sig = map(
            S, ("mx_w", "mx_bc", "mx_mixed", "mx_x2", "mx_sq", "mx_ms", "mx_root", "mx_h2", "mx_stored", "mx_t",
                "mx_t_ev", "mx_logits", "mx_sig"))
        x_loaded = [S("mx_x0"), S("mx_x1")]
        mT, h2T, x2, score = self.mT, self.h2T, self.x2, self.score
        flat = self.mod_rows.rearrange("r p -> (r p)")
        with ExitStack() as st:
            sb = lambda n, s, d=F32: st.enter_context(nc.sbuf_tensor(n, s, d))
            ps = lambda n, s, d=F32: st.enter_context(nc.psum_tensor(n, s, d))
            w = sb("wmix", [P, KT, D])
            wr = sb("wr", [P, KT, NE])
            bc = sb("mx_bcast", [P, 2, 3, D])
            x = sb("mx_xb", [P, 2, D])
            h2 = sb("mx_h2b", [P, 2, D])
            junk = sb("mx_junk", [P, D])
            ss, m, r, ri = (sb(f"mx_{n}", [P, NT]) for n in ("ss", "m", "r", "ri"))
            pm = [ps(f"mx_pm{i}", [P, 2, 512]) for i in range(2)]
            pt = ps("mx_pt", [P, 2, 512])
            pl = [ps(f"mx_pl{i}", [P, 512])[:, 0:NE] for i in range(2)]
            with nc.Block() as block:
                @block.sync
                def _(sp):
                    sp.dma_start(w[:, :, :], I["w_mix_out"][0].rearrange("(k p) n -> p k n", p=P)).then_inc(w_loaded, 16)
                    for g in range(2):
                        for n, v in enumerate((G1, SH2, SC2)):
                            at = (g * 48 + v * 8) * P
                            sp.dma_start(bc[:, g, n, :], flat[at:at + D].partition_broadcast(P)).then_inc(bc_loaded, 16)
                    sp.dma_start(wr[:, :, :], I["w_router"][0].rearrange("(k p) n -> p k n", p=P)).then_inc(w_loaded, 16)
                    for t in range(NT):
                        R = rows_of(t)
                        if t >= 2:
                            sp.wait_ge(x2_done, t - 1)
                        sp.dma_start(x[:R, t % 2, :], self.x_rows(t)).then_inc(x_loaded[t % 2], 16)
                        if t:
                            self.store_h2(sp, t - 1, h2, h2_ready, h2_stored)
                    self.store_h2(sp, NT - 1, h2, h2_ready, h2_stored)
                    sp.wait_ge(h2_stored, 16 * NT)

                @block.tensor
                def _(pe):
                    def trans(t):
                        R = rows_of(t)
                        pe.wait_ge(h2_ready, t + 1)
                        if t:
                            pe.wait_ge(t_ev, t)
                        for k in range(KT):
                            last = pe.transpose(pt[:, k // 4, (k % 4) * P:(k % 4) * P + R],
                                                h2[:R, t % 2, k * P:(k + 1) * P], self.ident[:R, :R])
                        last.then_inc(t_done, 1)

                    def logits(t):
                        R = rows_of(t)
                        pe.wait_ge(t_ev, t + 1)
                        if t >= 2:
                            pe.wait_ge(sig, t - 1)
                        for k in range(KT):
                            last = pe.matmul(pl[t % 2][:R, :], h2T[:, k, t * P:t * P + R], wr[:, k, :],
                                             start=(k == 0), stop=(k == KT - 1))
                        last.then_inc(lg, 1)

                    pe.wait_ge(w_loaded, 32)
                    for t in range(NT):
                        R = rows_of(t)
                        if t >= 2:
                            pe.wait_ge(x2_done, t - 1)
                        for k in range(KT):
                            for h in range(2):
                                last = pe.matmul(pm[t % 2][:R, h, :], mT[:, k, t * P:t * P + R], w[:, k, h * 512:(h + 1) * 512],
                                                 start=(k == 0), stop=(k == KT - 1))
                        last.then_inc(mixed, 1)
                        if t:
                            trans(t - 1)
                        if t >= 2:
                            logits(t - 2)
                    trans(NT - 1)
                    logits(NT - 2)
                    logits(NT - 1)

                @block.scalar
                def _(act):
                    link = self.link_of(act, "act")

                    def evac(t):
                        R = rows_of(t)
                        act.wait_ge(t_done, t + 1)
                        for h in range(2):
                            last = act.copy(h2T[:, 4 * h:4 * h + 4, t * P:t * P + R],
                                            pt[:, h, :].rearrange("p (k n) -> p k n", n=P)[:, :, 0:R])
                        last.then_inc(t_ev, 1)

                    def sigmoid(t):
                        R = rows_of(t)
                        act.wait_ge(lg, t + 1)
                        act.activation(score[:R, t, :], pl[t % 2][:R, :], ACT.Sigmoid).then_inc(sig, 1)

                    for t in range(NT):
                        R = rows_of(t)
                        act.wait_ge(x2_done, t + 1)
                        link(act.activation(junk[:R, :], x2[:R, t, :], ACT.Square, accum_out=ss[:R, t:t + 1]))
                        act.sem_inc(sq, 1)
                        act.wait_ge(ms, t + 1)
                        act.activation(r[:R, t:t + 1], m[:R, t:t + 1], ACT.Sqrt).then_inc(rt, 1)
                        if t:
                            evac(t - 1)
                        if t >= 2:
                            sigmoid(t - 2)
                    evac(NT - 1)
                    sigmoid(NT - 2)
                    sigmoid(NT - 1)

                @block.vector
                def _(dve):
                    link = self.link_of(dve, "dve")
                    dve.memset(score[CHUNK:P, NT - 1, :], 0.5)
                    dve.wait_ge(bc_loaded, 96)
                    for t in range(NT):
                        R = rows_of(t)
                        g = int(t == NT - 1)
                        dve.wait_ge(mixed, t + 1)
                        dve.wait_ge(x_loaded[t % 2], 16 * (t // 2 + 1))
                        link(dve.tensor_tensor(x2[:R, t, :].rearrange("p (a n) -> p a n", a=2), pm[t % 2][:R, :, :],
                                               bc[:R, g, 0, :].rearrange("p (a n) -> p a n", a=2), ALU.mult))
                        dve.tensor_tensor(x2[:R, t, :], x2[:R, t, :], x[:R, t % 2, :], ALU.add).then_inc(x2_done, 1)
                        dve.wait_ge(sq, t + 1)
                        dve.tensor_scalar(m[:R, t:t + 1], ss[:R, t:t + 1], 1.0 / D, EPS, ALU.mult, ALU.add).then_inc(ms, 1)
                        dve.wait_ge(rt, t + 1)
                        link(dve.reciprocal(ri[:R, t:t + 1], r[:R, t:t + 1]))
                        if t >= 2:
                            dve.wait_ge(h2_stored, 16 * (t - 1))
                            dve.wait_ge(t_done, t - 1)
                        link(dve.scalar_tensor_tensor(h2[:R, t % 2, :], x2[:R, t, :], ri[:R, t:t + 1], bc[:R, g, 2, :], ALU.mult, ALU.mult))
                        dve.tensor_tensor(h2[:R, t % 2, :], h2[:R, t % 2, :], bc[:R, g, 1, :], ALU.add).then_inc(h2_ready, 1)

    def store_h2(self, sp, t, h2, h2_ready, h2_stored):
        R = rows_of(t)
        sp.wait_ge(h2_ready, t + 1)
        sp.dma_start(self.h2_rows[t * P:t * P + R, :], h2[:R, t % 2, :]).then_inc(h2_stored, 16)

    def routing(self):
        nc, I = self.nc, self.I
        S = self.sem
        con, score = self.con, self.score
        place_w, place_x = self.place_w, self.place_x
        zeroed = S("rt_zeroed")
        bias_l, mask_ready, ranked, counted, nblk_ready, start_done, start_ev, cmp_ready, eb_done, hot, hot_used, tab = map(
            S, ("rt_bias", "rt_mask", "rt_ranked", "rt_counted", "rt_nblk", "rt_start", "rt_start_ev", "rt_cmp",
                "rt_eb", "rt_hot", "rt_hot_used", "rt_table"))
        NR = NT * NE
        with ExitStack() as st:
            sb = lambda n, s, d=F32: st.enter_context(nc.sbuf_tensor(n, s, d))
            ps = lambda n, s, d=F32: st.enter_context(nc.psum_tensor(n, s, d))
            bias = sb("rt_biasb", [P, NE])
            biased = sb("biased", [P, NT, NE])
            top = sb("rt_top", [P, NT * NG, 8])
            gsc = sb("gsc", [P, NT, NG])
            cmpg = sb("cmpg", [P, NT * NG, NG])
            eqg = sb("eqg", [P, NT * NG, NG])
            grank = sb("grank", [P, NT * NG])
            gmask = sb("gmask", [P, NT * NG])
            gneg = sb("gneg", [P, NT * NG])
            masked = sb("rt_masked", [P, NT, NE])
            best = sb("best", [P, NT, 8])
            rep = sb("rep", [P, NT, NE])
            mask = sb("mask", [P, NT, NE])
            maskh = sb("maskh", [P, NT, NE], BF16)
            trih = sb("trih", [P, P], BF16)
            oneh = sb("oneh", [P, P], BF16)
            wd = sb("wd", [P, NT, NE])
            wsum = sb("wsum", [P, NT])
            rsum = sb("rsum", [P, NT])
            cnt = sb("cnt", [NE, 1])
            over = sb("over", [NE, NTHR])
            nblk = sb("nblk", [NE, 1])
            nblkh = sb("nblkh", [NE, P], BF16)
            nzh = sb("nzh", [NE, 1], BF16)
            enzh = sb("enzh", [NE, 1], BF16)
            nz = sb("nz", [NE, 1])
            ordc = sb("ordc", [NE, 1])
            ohw = sb("ohw", [NE, NE], BF16)
            ordf = sb("ordf", [1, NBP])
            chg = sb("chg", [1, NBP])
            usedf = sb("usedf", [1, 1])
            startc = sb("startc", [NE, 1])
            startr = sb("startr", [P, NE])
            cmpb = sb("cmpb", [NE, NBP], BF16)
            key = sb("key", [P, NT, NE])
            key8 = sb("key8", [P, NT, 8])
            eq8 = sb("eq8", [P, 8, NE])
            slot = sb("slot", [P, NT * 8])
            sloti = sb("sloti", [P, NT * 8], I32)
            lo = sb("lo", [P, NT * 8], I32)
            hi = sb("hi", [P, NT * 8], I32)
            lof = sb("lof", [P, NT * 8])
            hif = sb("hif", [P, NT * 8])
            w8 = sb("w8", [P, NT, TOPK])
            hp = sb("hot_p", [P, 4, P])
            hc = sb("hot_c", [P, 4, 2, NCOL])
            zero = sb("rt_zero", [P, D])
            tabf = sb("tabf", [P, NCOL])
            miss = sb("miss", [P, NCOL])
            pr = [ps(f"rt_pr{i}", [P, 8, NE]) for i in range(2)]
            pc = ps("rt_pc", [NE, 512])[:, 0:1]
            psr = ps("rt_psr", [P, 512])[:, 0:NE]
            psc = ps("rt_psc", [NE, 512])[:, 0:2]
            pst = ps("rt_pst", [P, 512])[:, 0:2]
            peb = ps("rt_peb", [1, 512])
            ptb = ps("rt_ptb", [P, 512])[:, 0:2 * NCOL].rearrange("p (a n) -> p a n", a=2)
            rank = lambda t: pr[t // 8][:, t % 8, :]
            with nc.Block() as block:
                @block.sync
                def _(sp):
                    sp.dma_start(bias[:, :], I["router_bias"][0].partition_broadcast(P)).then_inc(bias_l, 16)
                    sp.wait_ge(zeroed, 1)
                    for t in range(NT):
                        sp.dma_start(self.sum_rows[t * P:t * P + rows_of(t), :], zero[:rows_of(t), :]).then_inc(self.sum_cleared, 16)

                @block.vector
                def _(dve):
                    link = self.link_of(dve, "dve")
                    link(dve.tensor_copy(trih[:, :], con[:, C_TRI:C_TRI + P]))
                    link(dve.memset(oneh[:, :], 1.0))
                    dve.memset(zero[:, :], 0.0).then_inc(zeroed, 1)
                    dve.wait_ge(bias_l, 16)
                    link(dve.tensor_tensor(biased[:, :, :], score[:, :, :],
                                           bias[:, :].unsqueeze(1).to_broadcast([P, NT, NE]), ALU.add))
                    for t in range(NT):
                        for g in range(NG):
                            last = dve.max(top[:, t * NG + g, :], biased[:, t, g * GS:(g + 1) * GS])
                    link(last)
                    gs2 = gsc[:, :, :].rearrange("p t g -> p (t g)")
                    link(dve.tensor_tensor(gs2, top[:, :, 0], top[:, :, 1], ALU.add))
                    for t in range(NT):
                        a = gsc[:, t, :].unsqueeze(1).to_broadcast([P, NG, NG])
                        b = gsc[:, t, :].unsqueeze(2).to_broadcast([P, NG, NG])
                        dve.tensor_tensor(cmpg[:, t * NG:(t + 1) * NG, :], a, b, ALU.is_gt)
                        last = dve.tensor_tensor(eqg[:, t * NG:(t + 1) * NG, :], a, b, ALU.is_equal)
                    link(last)
                    low = con[:, C_LOW:C_LOW + NG * NG].rearrange("p (g h) -> p g h", h=NG)
                    for t in range(NT):
                        v = eqg[:, t * NG:(t + 1) * NG, :]
                        last = dve.tensor_tensor(v, v, low, ALU.mult)
                    link(last)
                    link(dve.tensor_tensor(cmpg[:, :, :], cmpg[:, :, :], eqg[:, :, :], ALU.add))
                    link(dve.tensor_reduce(grank[:, :], cmpg[:, :, :], AX.X, ALU.add))
                    link(dve.tensor_scalar(gmask[:, :], grank[:, :], float(TOPG), None, ALU.is_lt))
                    link(dve.tensor_scalar(gneg[:, :], gmask[:, :], -1.0, 1e30, ALU.add, ALU.mult))
                    m3 = masked[:, :, :].rearrange("p t (g e) -> p (t g) e", e=GS)
                    b3 = biased[:, :, :].rearrange("p t (g e) -> p (t g) e", e=GS)
                    link(dve.tensor_tensor(m3, b3, gmask[:, :].unsqueeze(2).to_broadcast([P, NT * NG, GS]), ALU.mult))
                    link(dve.tensor_tensor(m3, m3, gneg[:, :].unsqueeze(2).to_broadcast([P, NT * NG, GS]), ALU.add))
                    for t in range(NT):
                        last = dve.max(best[:, t, :], masked[:, t, :])
                    link(last)
                    for t in range(NT):
                        last = dve.match_replace(rep[:, t, :], best[:, t, :], masked[:, t, :], -3e38)
                    link(last)
                    link(dve.tensor_tensor(mask[:, :, :], rep[:, :, :], masked[:, :, :], ALU.not_equal))
                    link(dve.tensor_tensor(wd[:, :, :], mask[:, :, :], score[:, :, :], ALU.mult))
                    link(dve.tensor_reduce(wsum[:, :], wd[:, :, :], AX.X, ALU.add))
                    link(dve.reciprocal(rsum[:, :], wsum[:, :]))
                    for t in range(NT):
                        last = dve.tensor_scalar(wd[:, t, :], wd[:, t, :], rsum[:, t:t + 1], ROUTED_SCALE, ALU.mult, ALU.mult)
                    link(last)
                    link(dve.memset(mask[CHUNK:P, NT - 1, :], 0.0))
                    link(dve.tensor_copy(maskh[:, :, :], mask[:, :, :]))
                    dve.sem_inc(mask_ready, 1)
                    dve.wait_ge(counted, 1)
                    link(dve.tensor_copy(cnt[:, :], pc[:, :]))
                    link(dve.tensor_scalar(over[:, :], con[0:NE, C_THR:C_THR + NTHR], cnt[:, 0:1], None, ALU.is_lt))
                    link(dve.tensor_reduce(nblk[:, :], over[:, :], AX.X, ALU.add))
                    link(dve.tensor_scalar(nz[:, :], nblk[:, :], 0.0, None, ALU.is_gt))
                    link(dve.tensor_copy(nzh[:, :], nz[:, :]))
                    link(dve.tensor_tensor(enzh[:, :], nz[:, :], con[0:NE, C_ROW:C_ROW + 1], ALU.mult))
                    dve.tensor_copy(nblkh[:, :], nblk[:, 0:1].to_broadcast([NE, P])).then_inc(nblk_ready, 1)
                    dve.wait_ge(start_done, 1)
                    link(dve.tensor_copy(startr[:, :], psr[:, :]))
                    link(dve.tensor_copy(startc[:, :], psc[:, 0:1]))
                    link(dve.tensor_copy(ordc[:, :], psc[:, 1:2]))
                    link(dve.tensor_copy(self.n_blocks[:, :], pst[0:1, 0:1]))
                    link(dve.tensor_copy(self.n_used[:, :], pst[0:1, 1:2]))
                    link(dve.tensor_copy(usedf[:, :], pst[0:1, 1:2]))
                    link(dve.tensor_scalar(ohw[:, :], con[0:NE, C_IB:C_IB + NE], ordc[:, 0:1], None, ALU.is_equal))
                    dve.tensor_scalar(cmpb[:, :], con[0:NE, C_IB:C_IB + NBP], startc[:, 0:1], None, ALU.is_ge).then_inc(cmp_ready, 1)
                    dve.wait_ge(eb_done, 1)
                    link(dve.tensor_scalar(ordf[:, :], peb[:, 0:NBP], -1.0, None, ALU.add))
                    link(dve.tensor_copy(self.ord_e[:, :], peb[:, 256:256 + NE]))
                    link(dve.tensor_copy(self.blk_ord[:, :], ordf[:, :]))
                    link(dve.memset(chg[:, :], 1.0))
                    link(dve.tensor_tensor(chg[:, 1:NBP], ordf[:, 1:NBP], ordf[:, 0:NBP - 1], ALU.not_equal))
                    link(dve.tensor_scalar(ordf[:, :], ordf[:, :], 1.0, None, ALU.add))
                    link(dve.scalar_tensor_tensor(chg[:, :], ordf[:, :], usedf[:, 0:1], chg[:, :], ALU.is_lt, ALU.mult))
                    link(dve.tensor_tensor(self.blk_split[:, :], chg[:, :], ordf[:, :], ALU.mult))
                    dve.wait_ge(ranked, 1)
                    for t in range(NT):
                        last = dve.scalar_tensor_tensor(key[:, t, :], startr[:, :], float(BLK), rank(t), ALU.mult, ALU.add)
                    link(last)
                    link(dve.tensor_scalar(key[:, :, :], key[:, :, :], -1.0, KEY0, ALU.mult, ALU.add))
                    link(dve.tensor_tensor(key[:, :, :], key[:, :, :], mask[:, :, :], ALU.mult))
                    for t in range(NT):
                        last = dve.max(key8[:, t, :], key[:, t, :])
                    link(last)
                    link(dve.tensor_scalar(slot[:, :], key8[:, :, :].rearrange("p t j -> p (t j)"), -1.0, KEY0, ALU.mult, ALU.add))
                    link(dve.tensor_copy(sloti[:, :], slot[:, :]))
                    dve.tensor_single_scalar(lo[:, :], sloti[:, :], P - 1, ALU.bitwise_and)
                    link(dve.tensor_single_scalar(hi[:, :], sloti[:, :], 7, ALU.logical_shift_right))
                    dve.tensor_copy(lof[:, :], lo[:, :])
                    link(dve.tensor_copy(hif[:, :], hi[:, :]))
                    for t in range(NT):
                        link(dve.tensor_tensor(eq8[:, :, :], key[:, t, :].unsqueeze(1).to_broadcast([P, 8, NE]),
                                               key8[:, t, :].unsqueeze(2).to_broadcast([P, 8, NE]), ALU.is_equal))
                        link(dve.tensor_tensor(eq8[:, :, :], eq8[:, :, :], wd[:, t, :].unsqueeze(1).to_broadcast([P, 8, NE]), ALU.mult))
                        link(dve.tensor_reduce(w8[:, t, :], eq8[:, :, :], AX.X, ALU.add))
                    for n in range(NT * TOPK):
                        if n >= 4:
                            dve.wait_ge(hot_used, n - 3)
                        dve.tensor_scalar(hp[:, n % 4, :], con[:, C_IP:C_IP + P], lof[:, n:n + 1], None, ALU.is_equal)
                        dve.tensor_scalar(hc[:, n % 4, 0, :], con[:, C_IC:C_IC + NCOL], hif[:, n:n + 1],
                                          con[:, C_VAL + n:C_VAL + n + 1], ALU.is_equal, ALU.mult)
                        dve.tensor_scalar(hc[:, n % 4, 1, :], con[:, C_IC:C_IC + NCOL], hif[:, n:n + 1],
                                          w8[:, n // TOPK, n % TOPK:n % TOPK + 1], ALU.is_equal, ALU.mult).then_inc(hot, 1)
                    dve.wait_ge(tab, 1)
                    link(dve.tensor_copy(tabf[:, :], ptb[:, 0, :]))
                    link(dve.tensor_copy(place_w[:, :], ptb[:, 1, :]))
                    link(dve.tensor_scalar(miss[:, :], tabf[:, :], 0.0, NOWHERE, ALU.is_equal, ALU.mult))
                    link(dve.scalar_tensor_tensor(tabf[:, :], tabf[:, :], -1.0, miss[:, :], ALU.add, ALU.add))
                    link(dve.tensor_scalar(tabf[:, :], tabf[:, :], NOWHERE, None, ALU.min))
                    link(dve.tensor_copy(place_x[:, :], tabf[:, :]))

                @block.tensor
                def _(pe):
                    pe.wait_ge(mask_ready, 1)
                    for t in range(NT):
                        last = pe.matmul(pc[:, :], maskh[:, t, :], oneh[:, 0:1], start=(t == 0), stop=(t == NT - 1))
                    last.then_inc(counted, 1)
                    for t in range(NT):
                        last = pe.matmul(rank(t), trih[:, :], maskh[:, t, :], start=True, stop=(t == 0))
                        for b in range(t):
                            last = pe.matmul(rank(t), oneh[:, :], maskh[:, b, :], start=False, stop=(b == t - 1))
                    last.then_inc(ranked, 1)
                    pe.wait_ge(nblk_ready, 1)
                    pe.matmul(psr[:, :], nblkh[:, :], trih[0:NE, 0:NE], start=True, stop=True)
                    pe.matmul(psc[:, 0:1], trih[0:NE, 0:NE], nblkh[:, 0:1], start=True, stop=True)
                    pe.matmul(psc[:, 1:2], trih[0:NE, 0:NE], nzh[:, :], start=True, stop=True)
                    pe.matmul(pst[:, 0:1], oneh[0:NE, :], nblkh[:, 0:1], start=True, stop=True)
                    pe.matmul(pst[:, 1:2], oneh[0:NE, :], nzh[:, :], start=True, stop=True).then_inc(start_done, 1)
                    pe.wait_ge(cmp_ready, 1)
                    pe.matmul(peb[:, 0:NBP], nzh[:, :], cmpb[:, :], start=True, stop=True)
                    pe.matmul(peb[:, 256:256 + NE], enzh[:, :], ohw[:, :], start=True, stop=True).then_inc(eb_done, 1)
                    for n in range(NT * TOPK):
                        pe.wait_ge(hot, n + 1)
                        pe.matmul(ptb[:, :, :], hp[:, n % 4, :], hc[:, n % 4, :, :], start=(n == 0), stop=(n == NT * TOPK - 1)).then_inc(hot_used, 1)
                    pe.wait_ge(hot_used, NT * TOPK)
                    pe.sem_inc(tab, 1)

    def shared(self):
        nc, I = self.nc, self.I
        S = self.sem
        wl, bl, job, sg, sa, ready, down, added = map(
            S, ("sh_w", "sh_bc", "sh_job", "sh_sig", "sh_a", "sh_ready", "sh_down", "sh_added"))
        h2T, x2 = self.h2T, self.x2
        flat = self.mod_rows.rearrange("r p -> (r p)")
        NF = DSH // P
        with ExitStack() as st:
            sb = lambda n, s, d=F32: st.enter_context(nc.sbuf_tensor(n, s, d))
            ps = lambda n, s, d=F32: st.enter_context(nc.psum_tensor(n, s, d))
            g2b = sb("sh_g2b", [P, 2, D])
            wg = sb("sh_wg", [P, KT, DSH])
            wu = sb("sh_wu", [P, KT, DSH])
            wd = sb("sh_wd", [P, NF, D])
            s_ = sb("sh_s", [P, NF, NCH, CH])
            a = sb("sh_ab", [P, NF, TOK])
            tmp = sb("sh_tmp", [P, 2, D])
            ph = [ps(f"sh_ph{i}", [P, 4, 512]) for i in range(2)]
            with nc.Block() as block:
                @block.sync
                def _(sp):
                    sp.dma_start(wg[:, :, :], I["w_sh_gate"][0].rearrange("(k p) n -> p k n", p=P)).then_inc(wl, 16)
                    sp.dma_start(wu[:, :, :], I["w_sh_up"][0].rearrange("(k p) n -> p k n", p=P)).then_inc(wl, 16)
                    sp.dma_start(wd[:, :, :], I["w_sh_down"][0].rearrange("(k p) n -> p k n", p=P)).then_inc(wl, 16)
                    for g in range(2):
                        at = (g * 48 + G2 * 8) * P
                        sp.dma_start(g2b[:, g, :], flat[at:at + D].partition_broadcast(P)).then_inc(bl, 16)
                    sp.wait_ge(bl, 32)

                @block.tensor
                def _(pe):
                    pe.wait_ge(wl, 48)
                    for f in range(NF):
                        for half, w in enumerate((wg, wu)):
                            if f:
                                pe.wait_ge(sa if half == 0 else ready, f)
                            for k in range(KT):
                                for c in range(NCH):
                                    last = pe.matmul(ph[half][:, c, 0:CH], w[:, k, f * P:(f + 1) * P], h2T[:, k, c * CH:(c + 1) * CH],
                                                     start=(k == 0), stop=(k == KT - 1))
                            last.then_inc(job, 1)
                    pe.wait_ge(ready, NF)
                    for t in range(NT):
                        R = rows_of(t)
                        if t >= 2:
                            pe.wait_ge(added, t - 1)
                        for f in range(NF):
                            for h in range(2):
                                last = pe.matmul(ph[t % 2][:R, h, :], a[:, f, t * P:t * P + R], wd[:, f, h * 512:(h + 1) * 512],
                                                 start=(f == 0), stop=(f == NF - 1))
                        last.then_inc(down, 1)

                @block.scalar
                def _(act):
                    for f in range(NF):
                        act.wait_ge(job, 2 * f + 1)
                        act.activation(s_[:, f, :, :], ph[0][:, :, 0:CH], ACT.Sigmoid).then_inc(sg, 1)

                @block.vector
                def _(dve):
                    for f in range(NF):
                        dve.wait_ge(sg, f + 1)
                        dve.tensor_tensor(s_[:, f, :, :], s_[:, f, :, :], ph[0][:, :, 0:CH], ALU.mult).then_inc(sa, 1)
                        dve.wait_ge(job, 2 * f + 2)
                        dve.wait_ge(sa, f + 1)
                        dve.tensor_tensor(a[:, f, :].rearrange("p (c n) -> p c n", n=CH), s_[:, f, :, :], ph[1][:, :, 0:CH], ALU.mult).then_inc(ready, 1)
                    dve.wait_ge(bl, 32)
                    link = self.link_of(dve, "dve")
                    for t in range(NT):
                        R = rows_of(t)
                        g = int(t == NT - 1)
                        dve.wait_ge(down, t + 1)
                        dve.tensor_tensor(tmp[:R, t % 2, :].rearrange("p (a n) -> p a n", a=2), ph[t % 2][:R, 0:2, :],
                                               g2b[:R, g, :].rearrange("p (a n) -> p a n", a=2), ALU.mult).then_inc(added, 1)
                        dve.wait_ge(added, t + 1)
                        link(dve.tensor_tensor(x2[:R, t, :], x2[:R, t, :], tmp[:R, t % 2, :], ALU.add))

    def experts(self):
        nc, I = self.nc, self.I
        S = self.sem
        NF = DE // P
        w_loaded = [S(f"ex_w{i}") for i in range(3)]
        rows_gathered, y_stored = S("ex_rows_gathered"), S("ex_y_stored")
        idx, turn, y_free = S("ex_index"), S("ex_turn"), S("ex_y_free")
        transposed = S("ex_transposed")
        x_hi, x_lo = S("ex_x_hi"), S("ex_x_lo")
        w_hi, w_lo = S("ex_w_hi"), S("ex_w_lo")
        gate_up, h_transposed = S("ex_gate_up"), S("ex_h_transposed")
        down = S("ex_down")
        sig_done, silu_done, hidden = S("ex_sigmoid"), S("ex_silu"), S("ex_hidden")
        h_hi, h_lo = S("ex_h_hi"), S("ex_h_lo")
        y_ready = S("ex_y_ready")
        srcs = (I["w_exp_gate"][0], I["w_exp_up"][0], I["w_exp_down"][0])
        place_x, place_w = self.place_x, self.place_w
        with ExitStack() as st:
            sb = lambda n, s, d=F32: st.enter_context(nc.sbuf_tensor(n, s, d))
            ps = lambda n, s, d=F32: st.enter_context(nc.psum_tensor(n, s, d))
            PIECE = KT * DE
            stage = [sb(f"ex_stage{i}", [P, PIECE]) for i in range(3)]
            wgu = [sb(f"ex_wgu_{n}", [P, 2, KT, 2 * DE], F32R) for n in ("hi", "lo")]
            wdn = [sb(f"ex_wdn_{n}", [P, 2, NF * D], F32R) for n in ("hi", "lo")]
            xr = sb("ex_rows", [P, D])
            ixx = sb("ex_index_gather", [P, 1], I32)
            ixy = sb("ex_index_scatter", [P, 1], I32)
            wcol = sb("ex_place_weights", [P, 1])
            xT = [sb(f"ex_xT_{n}", [P, KT, P], F32R) for n in ("hi", "lo")]
            s_ = sb("ex_s", [P, DE])
            h = sb("ex_h", [P, DE])
            hT = [sb(f"ex_hT_{n}", [P, NF, P], F32R) for n in ("hi", "lo")]
            y = sb("ex_y", [P, 2, 512])
            pt = [ps(f"ex_pt{i}", [P, 4, P]) for i in range(2)]
            pgu = ps("ex_pgu", [P, 2 * DE])
            py = [ps(f"ex_py{j}", [P, 512]) for j in range(2)]
            ph = ps("ex_ph", [P, 512])[:, 0:NF * P].rearrange("p (f n) -> p f n", f=NF)
            PASSES = ((0, 0), (0, 1), (1, 0))

            def blocks_of(eng):
                return eng.value_load(self.n_blocks[0:1, 0:1], min_val=2, max_val=MAX_BLOCKS)

            def table(eng, t, at, top):
                return eng.value_load(t[0:1, bass.ds(at, 1)], min_val=0, max_val=top)

            with nc.Block() as block:
                @block.sync
                def _(sp):
                    n = sp.value_load(self.n_used[0:1, 0:1], min_val=2, max_val=NE)

                    def load(w, waits):
                        e = table(sp, self.ord_e, w, NE - 1)
                        for p in range(3):
                            if waits is not None:
                                sp.wait_ge(w_lo, waits + 2 * (p + 1))
                            k = KT if p < 2 else NF
                            sp.dma_start(stage[p][:, :].rearrange("p (k n) -> p k n", k=k),
                                         srcs[p][bass.ds(e, 1)].rearrange("e (k p) n -> p (e k) n", p=P)).then_inc(w_loaded[p], 16)

                    load(0, None)
                    with sp.Fori(0, n - 1) as i:
                        load(i + 1, i * 6)

                @block.gpsimd
                def _(pool):
                    n = blocks_of(pool)

                    def gather():
                        pool.indirect_dma_start(xr[:, :], None, self.h2_rows, bass.IndirectOffsetOnAxis(ap=ixx[:, 0:1], axis=0),
                                                bounds_check=TOK - 1, oob_is_err=False).then_inc(rows_gathered, 16)

                    def wait(sem, value):
                        pool.wait_ge(sem, value)
                        pool.sem_inc(turn, 1)

                    pool.dma_start(xr[:, :], self.h2_rows[0:P, :]).then_inc(y_stored, 16)
                    pool.tensor_copy(ixx[:, :], place_x[:, 0:1]).then_inc(idx, 1)
                    pool.wait_ge(idx, 1)
                    pool.wait_ge(y_stored, 16)
                    gather()
                    for b in (1, 2):
                        pool.wait_ge(transposed, 2 * b)
                        pool.tensor_copy(ixx[:, :], place_x[:, b:b + 1]).then_inc(idx, 1)
                        pool.wait_ge(idx, b + 1)
                        gather()
                    pool.wait_ge(self.sum_cleared, 16 * NT)

                    def scatter(b, count):
                        wait(y_stored, b * 16 + 16)
                        pool.tensor_copy(wcol[:, :], place_w[:, bass.ds(b, 1)]).then_inc(y_free, 1)
                        pool.tensor_copy(ixy[:, :], place_x[:, bass.ds(b, 1)]).then_inc(idx, 1)
                        wait(idx, count)
                        wait(y_ready, b * 2 + 6)
                        pool.indirect_dma_start(self.sum_rows, bass.IndirectOffsetOnAxis(ap=ixy[:, 0:1], axis=0),
                                                y[:, :, :].rearrange("p a n -> p (a n)"), None,
                                                bounds_check=TOK - 1, oob_is_err=False,
                                                compute_op=ALU.add).then_inc(y_stored, 16)

                    with pool.Fori(0, n - 1) as i:
                        wait(transposed, i * 2 + 6)
                        pool.tensor_copy(ixx[:, :], place_x[:, bass.ds(i + 3, 1)]).then_inc(idx, 1)
                        wait(idx, i * 2 + 4)
                        gather()
                        scatter(i, i * 2 + 5)
                    scatter(n - 1, n * 2 + 2)
                    wait(rows_gathered, n * 16 + 32)
                    wait(y_stored, n * 16 + 16)

                @block.tensor
                def _(pe):
                    n = blocks_of(pe)

                    def rows(b, lo_value):
                        pe.wait_ge(rows_gathered, b * 16 + 16)
                        for r in range(2):
                            if lo_value is not None:
                                pe.wait_ge(x_lo, lo_value + r)
                            for k in range(4):
                                last = pe.transpose(pt[r][:, k, :], xr[:, (4 * r + k) * P:(4 * r + k + 1) * P], self.ident)
                            last.then_inc(transposed, 1)

                    def gates(b, ordinal, slot):
                        pe.wait_ge(x_lo, b * 2 + 2)
                        pe.wait_ge(w_lo, ordinal * 6 + 4)
                        for k in range(KT):
                            for a, c in PASSES:
                                w = wgu[c][:, bass.ds(slot, 1), k, :].rearrange("p s n -> p (s n)")
                                last = pe.matmul(pgu[:, :], xT[a][:, k, :], w, start=(k == 0 and (a, c) == PASSES[0]),
                                                 stop=(k == KT - 1 and (a, c) == PASSES[-1]))
                        last.then_inc(gate_up, 1)

                    def hiddens(b):
                        pe.wait_ge(hidden, b + 1)
                        for f in range(NF):
                            last = pe.transpose(ph[:, f, :], h[:, f * P:(f + 1) * P], self.ident)
                        last.then_inc(h_transposed, 1)

                    def downs(b, ordinal):
                        slot = ordinal % 2
                        pe.wait_ge(h_lo, b + 1)
                        pe.wait_ge(w_lo, ordinal * 6 + 6)
                        for j in range(2):
                            pe.wait_ge(y_ready, b * 2 + (j + 3))
                            for f in range(NF):
                                for a, c in PASSES:
                                    w = wdn[c][:, bass.ds(slot, 1), f * D + j * 512:f * D + (j + 1) * 512].rearrange("p s n -> p (s n)")
                                    last = pe.matmul(py[j][:, :], hT[a][:, f, :], w, start=(f == 0 and (a, c) == PASSES[0]),
                                                     stop=(f == NF - 1 and (a, c) == PASSES[-1]))
                            last.then_inc(down, 1)

                    pe.sem_inc(y_ready, 4)
                    pe.sem_inc(down, 2)
                    rows(0, None)
                    gates(0, 0, 0)
                    rows(1, 1)
                    hiddens(0)
                    before = pe.alloc_register("ordinal_of_block_before")
                    pe.reg_mov(before, 0)
                    with pe.Fori(0, n - 1) as i:
                        ordinal = table(pe, self.blk_ord, i + 1, NE - 1)
                        gates(i + 1, ordinal, ordinal % 2)
                        rows(i + 2, i * 2 + 3)
                        downs(i, pe.snap(before, min_val=0, max_val=NE - 1))
                        pe.reg_mov(before, ordinal)
                        hiddens(i + 1)
                    downs(n - 1, pe.snap(before, min_val=0, max_val=NE - 1))

                def halves(part, slot, p):
                    for q in range(2):
                        if p < 2:
                            k = slice(q * KT // 2, (q + 1) * KT // 2)
                            yield wgu[part][:, bass.ds(slot, 1), k, p * DE:(p + 1) * DE].rearrange("p s k n -> p (s k) n"), \
                                stage[p][:, :].rearrange("p (k n) -> p k n", k=KT)[:, k, :]
                        else:
                            n = slice(q * PIECE // 2, (q + 1) * PIECE // 2)
                            yield wdn[part][:, bass.ds(slot, 1), n].rearrange("p s n -> p (s n)"), stage[2][:, n]

                @block.scalar
                def _(act):
                    n = blocks_of(act)

                    def split(ordinal, slot, which):
                        for p in which:
                            act.wait_ge(w_loaded[p], ordinal * 16 + 16)
                            for dst, src in halves(0, slot, p):
                                act.copy(dst, src).then_inc(w_hi, 1)

                    def columns(b):
                        for r in range(2):
                            act.wait_ge(transposed, b * 2 + (r + 1))
                            act.copy(xT[0][:, 4 * r:4 * r + 4, :], pt[r][:, :, :]).then_inc(x_hi, 1)

                    def y_out(b):
                        act.wait_ge(y_free, b + 1)
                        for j in range(2):
                            act.wait_ge(down, b * 2 + (j + 3))
                            act.activation(y[:, j, :], py[j][:, :], ACT.Copy, scale=wcol[:, 0:1]).then_inc(y_ready, 1)

                    def sigmoid(b):
                        act.wait_ge(gate_up, b + 1)
                        act.activation(s_[:, :], pgu[:, 0:DE], ACT.Sigmoid).then_inc(sig_done, 1)

                    def hiddens(b):
                        act.wait_ge(h_transposed, b + 1)
                        act.copy(hT[0][:, :, :], ph[:, :, :]).then_inc(h_hi, 1)

                    columns(0)
                    split(0, 0, (0, 1, 2))
                    split(1, 1, (0, 1))
                    sigmoid(0)
                    columns(1)
                    hiddens(0)
                    split(1, 1, (2,))
                    with act.Fori(0, n - 1) as i:
                        following = table(act, self.blk_split, i + 1, NE - 1)
                        slot = following % 2
                        with act.If(following >= 1):
                            split(following, slot, (0, 1))
                        sigmoid(i + 1)
                        columns(i + 2)
                        y_out(i)
                        hiddens(i + 1)
                        with act.If(following >= 1):
                            split(following, slot, (2,))
                    y_out(n - 1)

                @block.vector
                def _(dve):
                    n = blocks_of(dve)

                    def split(ordinal, slot, which):
                        for p, q, (dst, src), (hi, _) in ((p, q, lo, hi) for p in which for q, (lo, hi) in
                                                          enumerate(zip(halves(1, slot, p), halves(0, slot, p)))):
                            dve.wait_ge(w_hi, ordinal * 6 + (2 * p + q + 1))
                            dve.tensor_tensor(dst, src, hi.bitcast(F32), ALU.subtract).then_inc(w_lo, 1)

                    def columns(b):
                        for r in range(2):
                            dve.wait_ge(x_hi, b * 2 + (r + 1))
                            dve.tensor_tensor(xT[1][:, 4 * r:4 * r + 4, :], pt[r][:, :, :], xT[0][:, 4 * r:4 * r + 4, :].bitcast(F32),
                                              ALU.subtract).then_inc(x_lo, 1)

                    def silu(b):
                        dve.wait_ge(sig_done, b + 1)
                        dve.tensor_tensor(s_[:, :], s_[:, :], pgu[:, 0:DE], ALU.mult).then_inc(silu_done, 1)
                        dve.wait_ge(silu_done, b + 1)
                        dve.tensor_tensor(h[:, :], s_[:, :], pgu[:, DE:2 * DE], ALU.mult).then_inc(hidden, 1)

                    def hiddens(b):
                        dve.wait_ge(h_hi, b + 1)
                        dve.tensor_tensor(hT[1][:, :, :], ph[:, :, :], hT[0][:, :, :].bitcast(F32), ALU.subtract).then_inc(h_lo, 1)

                    columns(0)
                    split(0, 0, (0, 1, 2))
                    split(1, 1, (0, 1))
                    silu(0)
                    columns(1)
                    hiddens(0)
                    split(1, 1, (2,))
                    with dve.Fori(0, n - 1) as i:
                        following = table(dve, self.blk_split, i + 1, NE - 1)
                        slot = following % 2
                        with dve.If(following >= 1):
                            split(following, slot, (0, 1))
                        silu(i + 1)
                        columns(i + 2)
                        hiddens(i + 1)
                        with dve.If(following >= 1):
                            split(following, slot, (2,))

    def combine(self):
        nc, I, O = self.nc, self.I, self.O
        S = self.sem
        gl, sq, ms, rt, gated, x3, o_ready = map(S, ("cb_gain", "cb_sq", "cb_ms", "cb_root", "cb_gated", "cb_x3", "cb_out"))
        y_loaded = [S(f"cb_y{i}") for i in range(4)]
        o_stored = [S("cb_st0"), S("cb_st1")]
        x2 = self.x2
        flat = self.mod_rows.rearrange("r p -> (r p)")
        with ExitStack() as st:
            sb = lambda n, s, d=F32: st.enter_context(nc.sbuf_tensor(n, s, d))
            gain = sb("cb_gainb", [P, D])
            g2b = sb("cb_g2b", [P, 2, D])
            y = sb("cb_y", [P, 4, D])
            junk = sb("cb_junk", [P, D])
            o = sb("cb_o", [P, 2, D])
            ss, m, r, ri = (sb(f"cb_{n}", [P, NT]) for n in ("ss", "m", "r", "ri"))
            with nc.Block() as block:
                @block.sync
                def _(sp):
                    sp.dma_start(gain[:, :], I["final_gain"].partition_broadcast(P)).then_inc(gl, 16)
                    for g in range(2):
                        at = (g * 48 + G2 * 8) * P
                        sp.dma_start(g2b[:, g, :], flat[at:at + D].partition_broadcast(P)).then_inc(gl, 16)
                    for t in range(NT):
                        R = rows_of(t)
                        if t >= 4:
                            sp.wait_ge(x3, t - 3)
                        sp.dma_start(y[:R, t % 4, :], self.sum_rows[t * P:t * P + R, :]).then_inc(y_loaded[t % 4], 16)
                        if t >= 4:
                            self.store_out(sp, t - 4, o, o_ready, o_stored)
                    for t in range(NT - 4, NT):
                        self.store_out(sp, t, o, o_ready, o_stored)
                    sp.wait_ge(o_stored[0], 16 * ((NT + 1) // 2))
                    sp.wait_ge(o_stored[1], 16 * (NT // 2))

                @block.vector
                def _(dve):
                    link = self.link_of(dve, "dve")

                    def out(t):
                        R = rows_of(t)
                        dve.wait_ge(rt, t + 1)
                        link(dve.reciprocal(ri[:R, t:t + 1], r[:R, t:t + 1]))
                        if t >= 2:
                            dve.wait_ge(o_stored[t % 2], 16 * (t // 2))
                        dve.scalar_tensor_tensor(o[:R, t % 2, :], x2[:R, t, :], ri[:R, t:t + 1], gain[:R, :], ALU.mult, ALU.mult).then_inc(o_ready, 1)

                    dve.wait_ge(gl, 48)
                    for t in range(NT):
                        R = rows_of(t)
                        g = int(t == NT - 1)
                        v = y[:R, t % 4, :]
                        dve.wait_ge(y_loaded[t % 4], 16 * (t // 4 + 1))
                        dve.tensor_tensor(v, v, g2b[:R, g, :], ALU.mult).then_inc(gated, 1)
                        dve.wait_ge(gated, t + 1)
                        dve.tensor_tensor(x2[:R, t, :], x2[:R, t, :], v, ALU.add).then_inc(x3, 1)
                        if t:
                            out(t - 1)
                        dve.wait_ge(sq, t + 1)
                        dve.tensor_scalar(m[:R, t:t + 1], ss[:R, t:t + 1], 1.0 / D, EPS, ALU.mult, ALU.add).then_inc(ms, 1)
                    out(NT - 1)

                @block.scalar
                def _(act):
                    link = self.link_of(act, "act")
                    for t in range(NT):
                        R = rows_of(t)
                        act.wait_ge(x3, t + 1)
                        link(act.activation(junk[:R, :], x2[:R, t, :], ACT.Square, accum_out=ss[:R, t:t + 1]))
                        act.sem_inc(sq, 1)
                        act.wait_ge(ms, t + 1)
                        act.activation(r[:R, t:t + 1], m[:R, t:t + 1], ACT.Sqrt).then_inc(rt, 1)

    def store_out(self, sp, t, o, o_ready, o_stored):
        R = rows_of(t)
        dst = self.O["y_prompt"][0, t * P:(t + 1) * P, :] if t < NT - 1 else self.O["y_sample"][0]
        sp.wait_ge(o_ready, t + 1)
        sp.dma_start(dst, o[:R, t % 2, :]).then_inc(o_stored[t % 2], 16)


_OUTS = [("y_prompt", (1, SEQ, D)), ("y_sample", (1, DEC, D)), ("prompt_conv", (1, 1, 2, D)),
         ("prompt_k", (1, 1, WINDOW, NKV, HD)), ("prompt_v", (1, 1, WINDOW, NKV, HD)),
         ("sample_conv", (1, 1, 2, D)), ("sample_k", (1, 1, WINDOW, NKV, HD)), ("sample_v", (1, 1, WINDOW, NKV, HD))]


def kernel(**inputs):
    import numpy as _np
    import concourse.bacc as _bacc
    from concourse.bass_utils import run_bass_kernel_spmd as _run

    nc = _bacc.Bacc("TRN2", target_bir_lowering=False, num_devices=1)
    arrays, ins = {}, {}
    inputs = dict(inputs)
    inputs["con"] = constants()
    for name, value in inputs.items():
        a = _np.ascontiguousarray(value)
        arrays[f"in_{name}"] = a
        ins[name] = nc.dram_tensor(f"in_{name}", a.shape, mybir.dt.from_np(a.dtype), kind="ExternalInput").ap()
    outs = {n: nc.dram_tensor(f"out_{n}", s, F32, kind="ExternalOutput").ap() for n, s in _OUTS}
    Program(nc, ins, outs).build()
    r = _run(nc, [arrays], core_ids=[0])
    return tuple(r.results[0][f"out_{n}"] for n, _ in _OUTS)
```

```python
import numpy as np
import concourse.bass as bass
from concourse import mybir
from contextlib import ExitStack

F32 = mybir.dt.float32
F32R = mybir.dt.float32r
BF16 = mybir.dt.bfloat16
I32 = mybir.dt.int32
ALU = mybir.AluOpType
ACT = mybir.ActivationFunctionType
AX = mybir.AxisListType

P = 128
D = 1024
KT = D // P
SEQ = 1024
DEC = 64
TOK = SEQ + DEC
NT = -(-TOK // P)
PAST = 512
CHUNK = 64
WINDOW = 128
NQ, NKV, HD = 16, 4, 64
HALF = HD // 2
SCALE = HD ** -0.5
NE, TOPK, NG, GS, TOPG = 64, 8, 8, 8, 4
DE = 256
DSH = 256
ROUTED_SCALE = 2.5
EPS = 1e-6
KVD = NKV * HD
C_B, C_C, C_X, C_Q, C_K, C_V, C_GC, C_GA = 0, 1024, 2048, 3072, 4096, 4352, 4608, 5632
D_IN = 6656
NCH, CH = 4, TOK // 4
BLK = P
MAX_BLOCKS = NE + (TOK * TOPK - NE) // BLK
NBP = MAX_BLOCKS + 5
NCOL = NBP
NTHR = -(-TOK // BLK)
KEY0 = 32768.0
NOWHERE = float(1 << 20)
SH1, SC1, G1, SH2, SC2, G2 = range(6)

C_ID = 0
C_TRI = C_ID + P
C_IP = C_TRI + P
C_IC = C_IP + P
C_VAL = C_IC + NCOL
C_THR = C_VAL + NT * TOPK
C_IB = C_THR + NTHR
C_LOW = C_IB + NBP
C_ROW = C_LOW + NG * NG
C_COS = C_ROW + 1
C_SIN = C_COS + NT * HALF
C_END = C_SIN + NT * HALF


def constants():
    c = np.zeros((P, C_END), np.float32)
    r = np.arange(P)
    c[:, C_ID:C_ID + P] = np.eye(P)
    c[:, C_TRI:C_TRI + P] = r[:, None] < r[None, :]
    c[:, C_IP:C_IP + P] = r[None, :]
    c[:, C_IC:C_IC + NCOL] = np.arange(NCOL)[None, :]
    t = np.arange(NT)[:, None] * P
    val = t[None] + r[:, None, None] + 1 + np.zeros((1, 1, TOPK))
    c[:, C_VAL:C_VAL + NT * TOPK] = val.reshape(P, -1)
    c[:, C_THR:C_THR + NTHR] = np.arange(NTHR)[None] * BLK
    c[:, C_IB:C_IB + NBP] = np.arange(NBP)[None]
    c[:, C_ROW] = r
    g = np.arange(NG)
    c[:, C_LOW:C_LOW + NG * NG] = (g[None, :] < g[:, None]).reshape(1, -1)
    pos = np.concatenate([np.arange(SEQ), PAST + np.arange(NT * P - SEQ)]).astype(np.float32)
    freq = (10000.0 ** (-np.arange(HALF) / HALF)).astype(np.float32)
    ang = (pos[:, None] * freq[None, :]).astype(np.float32).astype(np.float64)
    for at, f in ((C_COS, np.cos), (C_SIN, np.sin)):
        c[:, at:at + NT * HALF] = f(ang).reshape(NT, P, HALF).transpose(1, 0, 2).reshape(P, -1)
    return c


class Link:

    def __init__(self, eng, sem):
        self.eng, self.sem, self.n = eng, sem, 0

    def __call__(self, ins):
        self.n += 1
        ins.then_inc(self.sem, 1)
        self.eng.wait_ge(self.sem, self.n)


def rows_of(t):
    return P if t < NT - 1 else TOK - (NT - 1) * P


class Program:
    def __init__(self, nc, I, O):
        self.nc, self.I, self.O = nc, I, O
        self.top = ExitStack()
        self.links = {}

    def link_of(self, eng, name):
        if name not in self.links:
            self.links[name] = Link(eng, self.sem(f"chain_{name}"))
        self.links[name].eng = eng
        return self.links[name]

    def sem(self, name):
        return self.top.enter_context(self.nc.semaphore(name))

    def sb(self, name, shape, dt=F32):
        cm = self.nc.sbuf_tensor(name, shape, dt)
        t = cm.__enter__()
        self.live[name] = cm
        return t

    def alias(self, name, shape, dt):
        cm = self.nc.sbuf_tensor(name, shape, dt)
        t = cm.__enter__()
        cm.__exit__(None, None, None)
        return t

    def free(self, *names):
        for n in names:
            self.live.pop(n).__exit__(None, None, None)

    def build(self):
        nc = self.nc
        self.live = {}
        with self.top:
            self.con = self.sb("con", [P, C_END])
            self.ident = self.con[:, C_ID:C_ID + P]
            self.modcol = self.sb("modcol", [P, 2, 16])
            self.mod_rows = nc.dram_tensor("mod_rows", (96, P), F32, kind="Internal").ap()
            self.h2_rows = nc.dram_tensor("h2_rows", (TOK, D), F32, kind="Internal").ap()
            self.sum_rows = nc.dram_tensor("sum_rows", (TOK, D), F32, kind="Internal").ap()
            self.sum_cleared = self.sem("sum_cleared")
            self.loaded_con = self.sem("loaded_con")
            self.stored = self.sem("stored")
            self.n_stored = 0
            self.score = self.sb("score", [P, NT, NE])
            self.place_w = self.sb("place_w", [P, NCOL])
            self.place_x = self.sb("place_x", [P, NCOL], I32)
            self.blk_ord = self.sb("blk_ord", [1, NBP], I32)
            self.blk_split = self.sb("blk_split", [1, NBP], I32)
            self.ord_e = self.sb("ord_e", [1, NE], I32)
            self.n_blocks = self.sb("n_blocks", [1, 1], I32)
            self.n_used = self.sb("n_used", [1, 1], I32)
            early_late = self.sb("early_late", [P, NT * D])
            self.wqkv = early_late[:, 0:2 * KT * 512].rearrange("p (b k n) -> p b k n", b=2, k=KT)
            self.oT = early_late[:, 0:KT * TOK].rearrange("p (k n) -> p k n", k=KT)
            self.x2 = early_late[:, :].rearrange("p (t n) -> p t n", t=NT)
            self.h_lo = self.alias("h_lo", [P, KT, TOK], F32R)
            self.hT = self.sb("hT", [P, KT, TOK])
            self.h2T = self.hT
            self.ada_norm1()
            self.qT = self.sb("qT", [HD, 17, NQ, CHUNK])
            self.kT = self.sb("kT", [HD, NKV, SEQ + WINDOW + DEC])
            self.V2 = self.sb("V2", [P, 19, KVD])
            self.qkv()
            self.attention()
            self.free("V2", "kT", "qT")
            self.mix_w = self.alias("mix_w", [P, KT, TOK], F32)
            self.h_hi = self.sb("h_hi", [P, KT, TOK], F32R)
            self.cT = self.sb("cT_all", [P, KT, TOK])
            self.conv_branch()
            self.mT = self.sb("mT", [P, KT, TOK])
            self.merge()
            self.mix()
            self.free("mT", "cT_all", "h_hi")
            self.routing_and_shared()
            self.free("hT")
            self.experts()
            self.combine()

    def x_rows(self, t):
        return self.I["x_prompt"][0, t * P:(t + 1) * P, :] if t < NT - 1 else self.I["x_sample"][0]

    def ada_norm1(self):
        nc, I = self.nc, self.I
        S = self.sem
        c_loaded, b_loaded = S("c_loaded"), S("b_ada_loaded")
        w_first = [S("w_ada_first0"), S("w_ada_first1")]
        w_loaded = [S("w_ada_loaded0"), S("w_ada_loaded1")]
        c_sig, c_silu, chunk_done, row_done, mod_t, mod_col, mod_stored = map(
            S, ("c_sig", "c_silu", "ada_chunk", "ada_row", "mod_t", "mod_col", "mod_stored"))
        x_loaded = [S(f"x_loaded{i}") for i in range(3)]
        sq, ms, rt, xn_ready, xt, ev_a, ev_v = map(S, ("n1_sq", "n1_ms", "n1_root", "n1_xn", "n1_xt", "n1_ev_act", "n1_ev_dve"))
        self.wq_loaded = [S("wq_loaded0"), S("wq_loaded1")]
        w_ada = I["w_ada"][0]
        NC = 12
        FIRST = 4
        hT, mod = self.hT, self.modcol
        with ExitStack() as st:
            sb = lambda n, s, d=F32: st.enter_context(nc.sbuf_tensor(n, s, d))
            ps = lambda n, s, d=F32: st.enter_context(nc.psum_tensor(n, s, d))
            wbuf = sb("w_ada_buf", [P, 2, KT, 1024])
            c_ld = sb("c_ld", [P, 2, KT])
            c_sg = sb("c_sg", [P, 2, KT])
            cT = sb("cT", [P, KT, 2])
            mrow = sb("mrow", [2, NC, 512])
            x = sb("n1_x", [P, 3, D])
            xn = sb("n1_xn_b", [P, 2, D])
            junk = sb("n1_junk", [P, D])
            ss, m, r, ri = (sb(f"n1_{n}", [P, NT]) for n in ("ss", "m", "r", "ri"))
            pm = [ps(f"pm{i}", [2, 512]) for i in range(2)]
            pcol = ps("pcol", [P, 512])[:, 0:32].rearrange("p (j g) -> p j g", g=2)
            pt = [ps(f"n1_pt{i}", [P, 2, 512]) for i in range(2)]
            with nc.Block() as block:
                @block.sync
                def _(sp):
                    for g, c in enumerate(("c_prompt", "c_sample")):
                        sp.dma_start(c_ld[:, g, :], I[c][0].rearrange("(p k) -> p k", k=KT)).then_inc(c_loaded, 16)
                    for h in range(2):
                        sp.dma_start(wbuf[:, 0, :, h * 512:(h + 1) * 512], w_ada[:, h * 512:(h + 1) * 512]
                                     .rearrange("(p k) n -> p k n", k=KT)).then_inc(w_first[h], 16)
                    for v in range(1, 6):
                        if v >= 2:
                            sp.wait_ge(chunk_done, 2 * v - 2)
                        sp.dma_start(wbuf[:, v % 2], w_ada[:, v * 1024:(v + 1) * 1024]
                                     .rearrange("(p k) n -> p k n", k=KT)).then_inc(w_loaded[v % 2], 16)
                    for cb in range(2):
                        sp.dma_start(self.wqkv[:, cb], I["w_in"][0][:, C_Q + cb * 512:C_Q + (cb + 1) * 512]
                                     .rearrange("(k p) n -> p k n", p=P)).then_inc(self.wq_loaded[cb], 16)
                    sp.wait_ge(row_done, NC)
                    sp.dma_start(self.mod_rows.rearrange("(g j) p -> g (j p)", g=2), mrow[:, :, :].rearrange("g c n -> g (c n)")).then_inc(mod_stored, 16)
                    sp.wait_ge(mod_stored, 16)

                @block.gpsimd
                def _(pool):
                    for t in range(NT):
                        R = rows_of(t)
                        if t >= 3:
                            pool.wait_ge(xn_ready, t - 2)
                        pool.dma_start(x[:R, t % 3, :], self.x_rows(t)).then_inc(x_loaded[t % 3], 16)

                @block.scalar
                def _(act):
                    act.dma_start(mrow[:, :, :].rearrange("g c n -> g (c n)"), I["b_ada"][0].partition_broadcast(2)).then_inc(b_loaded, 16)
                    act.dma_start(self.con[:, :], I["con"]).then_inc(self.loaded_con, 16)
                    link = self.link_of(act, "act")
                    act.wait_ge(c_loaded, 32)
                    act.activation(c_sg[:, :, :], c_ld[:, :, :], ACT.Sigmoid).then_inc(c_sig, 1)

                    def norm(t):
                        R = rows_of(t)
                        act.wait_ge(x_loaded[t % 3], 16 * (t // 3 + 1))
                        link(act.activation(junk[:R, :], x[:R, t % 3, :], ACT.Square, accum_out=ss[:R, t:t + 1]))
                        act.sem_inc(sq, 1)
                        act.wait_ge(ms, t + 1)
                        act.activation(r[:R, t:t + 1], m[:R, t:t + 1], ACT.Sqrt).then_inc(rt, 1)

                    def evac(t):
                        g = int(t == NT - 1)
                        R = rows_of(t)
                        act.wait_ge(xt, t + 1)
                        for k in range(4):
                            last = act.activation(hT[:, k, t * P:t * P + R], pt[t % 2][:, 0, k * P:k * P + R],
                                                  ACT.Identity, bias=mod[:, g, 8 * SH1 + k:8 * SH1 + k + 1],
                                                  scale=mod[:, g, 8 * SC1 + k:8 * SC1 + k + 1])
                        last.then_inc(ev_a, 1)

                    norm(0)
                    norm(1)
                    act.wait_ge(mod_col, 1)
                    for t in range(NT):
                        evac(t)
                        if t + 2 < NT:
                            norm(t + 2)

                @block.vector
                def _(dve):
                    link = self.link_of(dve, "dve")

                    def norm(t):
                        R = rows_of(t)
                        dve.wait_ge(sq, t + 1)
                        dve.tensor_scalar(m[:R, t:t + 1], ss[:R, t:t + 1], 1.0 / D, EPS, ALU.mult, ALU.add).then_inc(ms, 1)
                        dve.wait_ge(rt, t + 1)
                        link(dve.reciprocal(ri[:R, t:t + 1], r[:R, t:t + 1]))
                        if t >= 2:
                            dve.wait_ge(xt, t - 1)
                        dve.tensor_scalar(xn[:R, t % 2, :], x[:R, t % 3, :], ri[:R, t:t + 1], None,
                                          ALU.mult).then_inc(xn_ready, 1)

                    def row(c):
                        dve.wait_ge(chunk_done, c + 1)
                        dve.scalar_tensor_tensor(mrow[:, c, :], pm[c % 2][:, :], 1.0 if c // 2 in (SC1, SC2) else 0.0,
                                                 mrow[:, c, :], ALU.add, ALU.add).then_inc(row_done, 1)

                    def evac(t):
                        g = int(t == NT - 1)
                        R = rows_of(t)
                        dve.wait_ge(xt, t + 1)
                        for k in range(4, 8):
                            last = dve.tensor_scalar(hT[:, k, t * P:t * P + R], pt[t % 2][:, 1, (k - 4) * P:(k - 4) * P + R],
                                                     mod[:, g, 8 * SC1 + k:8 * SC1 + k + 1],
                                                     mod[:, g, 8 * SH1 + k:8 * SH1 + k + 1], ALU.mult, ALU.add)
                        last.then_inc(ev_v, 1)

                    dve.wait_ge(c_sig, 1)
                    dve.tensor_tensor(cT[:, :, :].rearrange("p k g -> p g k"), c_ld[:, :, :], c_sg[:, :, :],
                                      ALU.mult).then_inc(c_silu, 1)
                    norm(0)
                    norm(1)
                    dve.wait_ge(b_loaded, 16)
                    for c in range(FIRST):
                        row(c)
                    dve.wait_ge(mod_t, 1)
                    link(dve.tensor_copy(mod[:, :, :], pcol[:, :, :].rearrange("p j g -> p g j")))
                    dve.sem_inc(mod_col, 1)
                    for t in range(NT):
                        evac(t)
                        if t + 2 < NT:
                            norm(t + 2)
                        if FIRST + t < NC:
                            row(FIRST + t)

                @block.tensor
                def _(pe):
                    def chunk(c):
                        if c < 2:
                            pe.wait_ge(w_first[c], 16)
                        elif c % 2 == 0:
                            pe.wait_ge(w_loaded[c // 2 % 2], 16 * ((c // 2 + 1) // 2))
                        if c >= 2:
                            pe.wait_ge(row_done, c - 1)
                        for k in range(KT):
                            last = pe.matmul(pm[c % 2][:, :], cT[:, k, :], wbuf[:, c // 2 % 2, k, c % 2 * 512:(c % 2 + 1) * 512],
                                             start=(k == 0), stop=(k == KT - 1))
                        last.then_inc(chunk_done, 1)

                    def tile(t):
                        R = rows_of(t)
                        pe.wait_ge(xn_ready, t + 1)
                        if t >= 2:
                            pe.wait_ge(ev_a, t - 1)
                            pe.wait_ge(ev_v, t - 1)
                        for k in range(KT):
                            last = pe.transpose(pt[t % 2][:, k // 4, (k % 4) * P:(k % 4) * P + R],
                                                xn[:R, t % 2, k * P:(k + 1) * P], self.ident[:R, :R])
                        last.then_inc(xt, 1)

                    pe.wait_ge(c_silu, 1)
                    for c in range(FIRST):
                        chunk(c)
                    pe.wait_ge(self.loaded_con, 16)
                    pe.wait_ge(row_done, FIRST)
                    for j in range(16):
                        last = pe.transpose(pcol[:, j, :], mrow[:, j // 4, j % 4 * P:(j % 4 + 1) * P], self.ident[0:2, 0:2])
                    last.then_inc(mod_t, 1)
                    for t in range(NT):
                        tile(t)
                        if FIRST + t < NC:
                            chunk(FIRST + t)

    def qkv(self):
        nc, I = self.nc, self.I
        S = self.sem
        w_loaded = self.wq_loaded
        proj, rot_done, roped, q_t, q_ev, v_ev, kc, kst, vst = map(
            S, ("qkv_proj", "qkv_read", "qkv_roped", "qkv_t", "qkv_ev", "qkv_v_ev", "kcache", "k_tail", "v_tail"))
        w_in = I["w_in"][0]
        kT, qT, V2, hT = self.kT, self.qT, self.V2, self.hT
        cos = self.con[:, C_COS:C_COS + NT * HALF].rearrange("p (t h) -> p t h", h=HALF)
        sin = self.con[:, C_SIN:C_SIN + NT * HALF].rearrange("p (t h) -> p t h", h=HALF)
        with ExitStack() as st:
            sb = lambda n, s, d=F32: st.enter_context(nc.sbuf_tensor(n, s, d))
            ps = lambda n, s, d=F32: st.enter_context(nc.psum_tensor(n, s, d))
            w = self.wqkv
            rot = sb("rot", [P, 2, 512])
            tsin = sb("tsin", [P, 512])
            kc_ld = sb("kc_ld", [P, KVD])
            kkeep = sb("kkeep", [P, 2, KVD])
            vkeep = sb("vkeep", [P, 2, KVD])
            pp = [ps(f"qk_pp{i}", [P, 512]) for i in range(2)]
            pt = [ps(f"qk_pt{i}", [HD, 8, P]) for i in range(2)]
            units = [(cb, t) for cb in range(3) for t in range(NT)]
            NU = len(units)
            with nc.Block() as block:
                @block.sync
                def _(sp):
                    sp.wait_ge(proj, NT)
                    sp.dma_start(w[:, 0], w_in[:, C_Q + 2 * 512:C_Q + 3 * 512]
                                 .rearrange("(k p) n -> p k n", p=P)).then_inc(w_loaded[0], 16)
                    sp.dma_start(kc_ld[:, :], I["cache_k"][0, 0].rearrange("w h d -> w (h d)")).then_inc(kc, 16)
                    sp.dma_start(V2[:, 16, :], I["cache_v"][0, 0].rearrange("w h d -> w (h d)")).then_inc(kc, 16)
                    O = self.O
                    keep = WINDOW - DEC
                    for o, c in (("sample_k", "cache_k"), ("sample_v", "cache_v")):
                        sp.dma_start(O[o][0, 0, 0:keep].rearrange("w h d -> w (h d)"),
                                     I[c][0, 0, DEC:WINDOW].rearrange("w h d -> w (h d)")).then_inc(self.stored, 16)
                    sp.wait_ge(kst, 2)
                    sp.wait_ge(vst, 2)
                    for g, (ok, ov) in enumerate((("prompt_k", "prompt_v"), ("sample_k", "sample_v"))):
                        a, b = (0, P) if g == 0 else (keep, WINDOW)
                        sp.dma_start(O[ok][0, 0, a:b].rearrange("w h d -> w (h d)"), kkeep[0:b - a, g, :]).then_inc(self.stored, 16)
                        sp.dma_start(O[ov][0, 0, a:b].rearrange("w h d -> w (h d)"), vkeep[0:b - a, g, :]).then_inc(self.stored, 16)
                    self.n_stored += 6
                    sp.wait_ge(self.stored, 16 * self.n_stored)
                    sp.wait_ge(kc, 32)

                @block.tensor
                def _(pe):
                    def transposes(u):
                        cb, t = units[u]
                        R = rows_of(t)
                        pe.wait_ge(roped, u + 1)
                        if u >= 2:
                            pe.wait_ge(q_ev, u - 1)
                        for h in range(8 if cb < 2 else 4):
                            last = pe.transpose(pt[u % 2][:, h, 0:R], rot[:R, u % 2, h * HD:(h + 1) * HD],
                                                self.ident[:R, :R])
                        last.then_inc(q_t, 1)

                    for u, (cb, t) in enumerate(units):
                        R = rows_of(t)
                        if t == 0:
                            pe.wait_ge(w_loaded[cb % 2], 16 * (cb // 2 + 1))
                        if u >= 2:
                            pe.wait_ge(rot_done, u - 1)
                            if units[u - 2][0] == 2:
                                pe.wait_ge(v_ev, u - 2 - 2 * NT + 1)
                        for k in range(KT):
                            last = pe.matmul(pp[u % 2][:R, :], hT[:, k, t * P:t * P + R], w[:, cb % 2, k, :],
                                             start=(k == 0), stop=(k == KT - 1))
                        last.then_inc(proj, 1)
                        if u:
                            transposes(u - 1)
                    transposes(NU - 1)
                    pe.wait_ge(kc, 32)
                    pe.wait_ge(q_ev, NU - 1)
                    for h in range(NKV):
                        last = pe.transpose(pt[NU % 2][:, h, :], kc_ld[:, h * HD:(h + 1) * HD], self.ident)
                    last.then_inc(q_t, 1)

                @block.vector
                def _(dve):
                    link = self.link_of(dve, "dve")
                    for u, (cb, t) in enumerate(units):
                        R = rows_of(t)
                        nh = 8 if cb < 2 else 4
                        dve.wait_ge(proj, u + 1)
                        if u >= 2:
                            dve.wait_ge(q_t, u - 1)
                        src = pp[u % 2][:R, 0:nh * HD].rearrange("p (h s d) -> p h s d", s=2, d=HALF)
                        ts = tsin[:R, 0:nh * HD].rearrange("p (h s d) -> p h s d", s=2, d=HALF)
                        dst = rot[:R, u % 2, 0:nh * HD].rearrange("p (h s d) -> p h s d", s=2, d=HALF)
                        c = cos[:R, t, :].unsqueeze(1).to_broadcast([R, nh, HALF])
                        s = sin[:R, t, :].unsqueeze(1).to_broadcast([R, nh, HALF])
                        for half in range(2):
                            dve.tensor_tensor(dst[:, :, half, :], src[:, :, half, :], c, ALU.mult)
                            last = dve.tensor_tensor(ts[:, :, half, :], src[:, :, 1 - half, :], s, ALU.mult)
                        link(last)
                        dve.sem_inc(rot_done, 1)
                        dve.tensor_tensor(dst[:, :, 0, :], dst[:, :, 0, :], ts[:, :, 0, :], ALU.subtract)
                        link(dve.tensor_tensor(dst[:, :, 1, :], dst[:, :, 1, :], ts[:, :, 1, :], ALU.add))
                        dve.sem_inc(roped, 1)
                        if cb == 2 and t >= NT - 2:
                            dve.tensor_copy(kkeep[:R, t - NT + 2, :], rot[:R, u % 2, 0:KVD]).then_inc(kst, 1)

                @block.scalar
                def _(act):
                    for u, (cb, t) in enumerate(units):
                        R = rows_of(t)
                        nch = R // CHUNK
                        if cb == 2:
                            act.wait_ge(rot_done, u + 1)
                            v = pp[u % 2][:R, KVD:2 * KVD]
                            if t >= NT - 2:
                                act.copy(vkeep[:R, t - NT + 2, :], v).then_inc(vst, 1)
                            if t < NT - 1:
                                act.copy(V2[:, 2 * t, :], v)
                                if t:
                                    act.copy(V2[CHUNK:P, 2 * t - 1, :], v[0:CHUNK])
                                last = act.copy(V2[0:CHUNK, 2 * t + 1, :], v[CHUNK:P])
                            else:
                                last = act.copy(V2[0:CHUNK, 18, :], v)
                            last.then_inc(v_ev, 1)
                        act.wait_ge(q_t, u + 1)
                        if cb < 2:
                            for c in range(nch):
                                last = act.copy(qT[:, 2 * t + c, cb * 8:cb * 8 + 8, :], pt[u % 2][:, :, c * CHUNK:(c + 1) * CHUNK])
                        else:
                            at = t * P if t < NT - 1 else SEQ + WINDOW
                            last = act.copy(kT[:, :, at:at + R], pt[u % 2][:, 0:NKV, 0:R])
                        last.then_inc(q_ev, 1)
                    act.wait_ge(q_t, NU + 1)
                    act.copy(kT[:, :, SEQ:SEQ + WINDOW], pt[NU % 2][:, 0:NKV, :]).then_inc(q_ev, 1)

    def attention(self):
        nc, I = self.nc, self.I
        S = self.sem
        sk, sc_done, mx, sexp, pn, t1d, ev1, ev2, od, oev, es_d = map(
            S, ("sink_loaded", "at_scores", "at_max", "at_exp", "at_probs", "at_t", "at_ev_act", "at_ev_dve",
                "at_o", "at_oev", "at_sinkdiff"))
        kT, qT, V2, oT = self.kT, self.qT, self.V2, self.oT
        units = [(n, hf) for n in range(17) for hf in range(2)]

        def keys(n):
            if n == 16:
                return SEQ, WINDOW, DEC, 16, 18
            if n == 0:
                return 0, CHUNK, 0, 0, None
            if n == 1:
                return 0, P, 0, 0, None
            return (n - 2) * CHUNK, P, CHUNK, n - 2, n

        with ExitStack() as st:
            sb = lambda n, s, d=F32: st.enter_context(nc.sbuf_tensor(n, s, d))
            ps = lambda n, s, d=F32: st.enter_context(nc.psum_tensor(n, s, d))
            sink = sb("sink", [P, 8])
            nsink = sb("nsink", [P, 8])
            m = sb("at_m", [P, 2, 4])
            nm = sb("at_nm", [P, 2, 4])
            ds_ = sb("at_ds", [P, 2, 4])
            es = sb("at_es", [P, 2, 4])
            rs = sb("at_rs", [P, 2, 4])
            z = sb("at_z", [P, 2, 4])
            rz = sb("at_rz", [P, 2, 4])
            pr = sb("at_p", [P, 2, 4, 192])
            pt1 = sb("at_pt1", [P, 2, 512])
            pt2 = sb("at_pt2", [CHUNK, 2, 512])
            sc = [ps(f"at_s{i}", [P, 2, 512]) for i in range(2)]
            p1 = ps("at_p1", [P, 512])
            p2 = ps("at_p2", [CHUNK, 512])
            po = [ps(f"at_po{i}", [CHUNK, 512]) for i in range(2)]
            with nc.Block() as block:
                @block.sync
                def _(sp):
                    for h in range(2):
                        src = I["attn_sinks"][0].rearrange("(j h) -> h j", h=2)[h:h + 1]
                        with nc.allow_non_contiguous_dma(reason="16 sinks"):
                            sp.dma_start(sink[h * CHUNK:(h + 1) * CHUNK, :], src.to_broadcast([CHUNK, 8])).then_inc(sk, 16)
                    sp.wait_ge(sk, 32)

                @block.tensor
                def _(pe):
                    def scores(u):
                        n, hf = units[u]
                        ks, a, b, _, _ = keys(n)
                        if u >= 2:
                            pe.wait_ge(sexp, u - 1)
                        for i in range(4):
                            j = hf * 4 + i
                            last = pe.matmul(sc[u % 2][:, i // 2, (i % 2) * 192:(i % 2) * 192 + a + b],
                                             qT[:, n, 2 * j:2 * j + 2, :], kT[:, j // 2, ks:ks + a + b],
                                             start=True, stop=True)
                        last.then_inc(sc_done, 1)

                    def transposes(u):
                        n, hf = units[u]
                        _, a, b, _, _ = keys(n)
                        pe.wait_ge(pn, u + 1)
                        if u:
                            pe.wait_ge(ev1, u)
                            pe.wait_ge(ev2, u)
                        for i in range(4):
                            last = pe.transpose(p1[0:a, i * P:(i + 1) * P], pr[:, u % 2, i, 0:a], self.ident)
                        if b:
                            for i in range(4):
                                last = pe.transpose(p2[:, i * P:(i + 1) * P], pr[:, u % 2, i, a:a + b], self.ident)
                        last.then_inc(t1d, 1)

                    def values(u):
                        n, hf = units[u]
                        _, a, b, va, vb = keys(n)
                        pe.wait_ge(ev1, u + 1)
                        pe.wait_ge(ev2, u + 1)
                        if u >= 2:
                            pe.wait_ge(oev, u - 1)
                        for i in range(2):
                            kv = (hf * 2 + i) * HD
                            last = pe.matmul(po[u % 2][:, i * 256:(i + 1) * 256], V2[0:a, va, kv:kv + HD],
                                             pt1[0:a, u % 2, i * 256:(i + 1) * 256], start=True, stop=(b == 0))
                            if b:
                                last = pe.matmul(po[u % 2][:, i * 256:(i + 1) * 256], V2[0:b, vb, kv:kv + HD],
                                                 pt2[0:b, u % 2, i * 256:(i + 1) * 256], start=False, stop=True)
                        last.then_inc(od, 1)

                    scores(0)
                    scores(1)
                    for u in range(len(units)):
                        if u + 2 < len(units):
                            scores(u + 2)
                        if u:
                            values(u - 1)
                        transposes(u)
                    values(len(units) - 1)

                @block.vector
                def _(dve):
                    link = self.link_of(dve, "dve")
                    dve.wait_ge(sk, 32)
                    link(dve.tensor_scalar(nsink[:, :], sink[:, :], -1.0, None, ALU.mult))

                    def head(u):
                        n, hf = units[u]
                        _, a, b, _, _ = keys(n)
                        b2 = u % 2
                        dve.wait_ge(sc_done, u + 1)
                        v = sc[b2][:, :, 0:384].rearrange("p b (a k) -> p b a k", a=2)[:, :, :, 0:a + b]
                        link(dve.tensor_reduce(m[:, b2, :].rearrange("p (b a) -> p b a", b=2), v, AX.X, ALU.max))
                        link(dve.scalar_tensor_tensor(nm[:, b2, :], m[:, b2, :], -SCALE, nsink[:, hf * 4:hf * 4 + 4], ALU.mult, ALU.min))
                        dve.tensor_tensor(ds_[:, b2, :], sink[:, hf * 4:hf * 4 + 4], nm[:, b2, :], ALU.add).then_inc(mx, 1)

                    def tail(u):
                        n, hf = units[u]
                        _, a, b, _, _ = keys(n)
                        b2 = u % 2
                        dve.wait_ge(sexp, u + 1)
                        link(dve.tensor_tensor(z[:, b2, :], rs[:, b2, :], es[:, b2, :], ALU.add))
                        link(dve.reciprocal(rz[:, b2, :], z[:, b2, :]))
                        dve.tensor_tensor(pr[:, b2, :, 0:a + b], pr[:, b2, :, 0:a + b],
                                          rz[:, b2, :].unsqueeze(2).to_broadcast([P, 4, a + b]), ALU.mult).then_inc(pn, 1)

                    def evac(u):
                        _, a, b, _, _ = keys(units[u][0])
                        dve.wait_ge(t1d, u + 1)
                        if u >= 2:
                            dve.wait_ge(od, u - 1)
                        if b:
                            dve.tensor_copy(pt2[:, u % 2, :], p2[:, :]).then_inc(ev2, 1)
                        else:
                            dve.sem_inc(ev2, 1)

                    head(0)
                    head(1)
                    for u in range(len(units)):
                        tail(u)
                        if u + 2 < len(units):
                            head(u + 2)
                        evac(u)

                @block.scalar
                def _(act):
                    link = self.link_of(act, "act")

                    def exps(u):
                        n, hf = units[u]
                        _, a, b, _, _ = keys(n)
                        b2 = u % 2
                        act.wait_ge(mx, u + 1)
                        if u >= 2:
                            act.wait_ge(t1d, u - 1)
                        act.activation(es[:, b2, :], ds_[:, b2, :], ACT.Exp)
                        for i in range(4):
                            last = act.activation(pr[:, b2, i, 0:a + b], sc[b2][:, i // 2, (i % 2) * 192:(i % 2) * 192 + a + b],
                                                  ACT.Exp, bias=nm[:, b2, i:i + 1], scale=SCALE, accum_out=rs[:, b2, i:i + 1])
                        last.then_inc(sexp, 1)

                    def evac(u):
                        n, hf = units[u]
                        _, a, b, _, _ = keys(n)
                        act.wait_ge(t1d, u + 1)
                        if u >= 2:
                            act.wait_ge(od, u - 1)
                        act.copy(pt1[0:a, u % 2, :], p1[0:a, :]).then_inc(ev1, 1)

                    def out(u):
                        n, hf = units[u]
                        act.wait_ge(od, u + 1)
                        v = po[u % 2][:, :].rearrange("p (j h q) -> p h j q", h=2, q=CHUNK)
                        act.copy(oT[0:CHUNK, hf * 4:hf * 4 + 4, n * CHUNK:(n + 1) * CHUNK], v[:, 0])
                        act.copy(oT[CHUNK:P, hf * 4:hf * 4 + 4, n * CHUNK:(n + 1) * CHUNK], v[:, 1]).then_inc(oev, 1)

                    exps(0)
                    exps(1)
                    for u in range(len(units)):
                        evac(u)
                        if u + 2 < len(units):
                            exps(u + 2)
                        if u:
                            out(u - 1)
                    out(len(units) - 1)

    def conv_branch(self):
        nc, I, O = self.nc, self.I, self.O
        S = self.sem
        LEN = SEQ + DEC + 4
        w_in = I["w_in"][0]
        w_loaded = [S(f"cv_w{i}") for i in range(3)]
        small, job, c_read, x_read, b_read, st_t, st_ev, tail_ready, tail_t, tail_ev = map(
            S, ("cv_small", "cv_job", "cv_c_read", "cv_x_read", "cv_b_read", "cv_state_t", "cv_state_ev",
                "cv_tail_ready", "cv_tail_t", "cv_tail_ev"))
        h_split_hi, h_split_lo, w_hi, w_lo = map(S, ("cv_h_hi", "cv_h_lo", "cv_w_hi", "cv_w_lo"))
        cT, hT = self.cT, self.hT
        h = (self.h_hi, self.h_lo)
        PASSES = ((0, 0), (0, 1), (1, 0))
        with ExitStack() as st:
            sb = lambda n, s, d=F32: st.enter_context(nc.sbuf_tensor(n, s, d))
            ps = lambda n, s, d=F32: st.enter_context(nc.psum_tensor(n, s, d))
            w = [sb(f"cv_wb{i}", [P, KT, P]) for i in range(3)]
            wp = [[sb(f"cv_w{n}{i}", [P, KT, P], F32R) for n in ("hi", "lo")] for i in range(3)]
            rows = sb("cv_rows", [40, P])
            wst = sb("cv_wst", [P, 40])
            cb = [sb(f"cv_c{i}", [P, TOK]) for i in range(2)]
            u = [sb(f"cv_u{i}", [P, LEN]) for i in range(2)]
            acc = sb("cv_acc", [P, LEN - 2])
            tail = sb("cv_tail", [P, 32])
            trow = sb("cv_trow", [32, P])
            ph = [ps(f"cv_ph{i}", [P, 4, 512]) for i in range(2)]
            COLS = (C_C, C_X, C_B)
            def pieces(half):
                p = ph[half]
                return ((0, p[:, 0:3, 0:CH], 0, 3 * CH), (3 * CH, p[:, 3, 0:SEQ - 3 * CH], 3 * CH, SEQ),
                        (SEQ + 2, p[:, 3, SEQ - 3 * CH:CH], SEQ, TOK))

            def cut(ap, n):
                return ap.rearrange("p (c n) -> p c n", n=CH) if n == 3 * CH else ap

            with nc.Block() as block:
                @block.sync
                def _(sp):
                    sp.dma_start(rows[0:24, :], I["w_conv"][0].rearrange("i (k p) -> (i k) p", p=P)).then_inc(small, 16)
                    sp.dma_start(rows[24:40, :], I["state_conv"][0, 0].rearrange("i (k p) -> (i k) p", p=P)).then_inc(small, 16)
                    def load(i, jj):
                        at = COLS[jj % 3] + jj // 3 * P
                        cols = slice(at, at + P) if isinstance(i, int) and i == 0 else bass.ds(i * 256 + at, P)
                        sp.dma_start(w[jj % 3][:, :, :], w_in[:, cols].rearrange("(k p) n -> p k n", p=P)).then_inc(w_loaded[jj % 3], 16)

                    for jj in range(3):
                        load(0, jj)

                    def step(i, jjs):
                        for jj in jjs:
                            sp.wait_ge(w_lo, i * 6 + (jj + 1))
                            load(i, jj + 3)

                    with sp.Fori(0, KT // 2 - 1) as i:
                        step(i, range(6))
                    step(KT // 2 - 1, range(3))
                    sp.wait_ge(tail_ev, 1)
                    for g, o in enumerate(("prompt_conv", "sample_conv")):
                        sp.dma_start(O[o][0, 0].rearrange("i (k p) -> (i k) p", p=P), trow[g * 16:(g + 1) * 16, :]).then_inc(self.stored, 16)
                    self.n_stored += 2
                    sp.wait_ge(self.stored, 16 * self.n_stored)

                @block.tensor
                def _(pe):
                    pe.wait_ge(small, 32)
                    pe.transpose(ph[0][:, 0, 0:40], rows[:, :], self.ident[0:40, 0:40]).then_inc(st_t, 1)
                    pe.wait_ge(st_ev, 1)
                    with pe.Fori(0, KT // 2) as i:
                        for s in range(2):
                            before = ((x_read, 0, 2), (b_read, 0, 2), (c_read, 1, 0)) if s == 0 else \
                                     ((x_read, 1, 2), (b_read, 1, 2), (c_read, 2, 0))
                            for x in range(3):
                                jj = 3 * s + x
                                sem, n, credit = before[x]
                                pe.wait_ge(sem, i * 2 + (n + credit))
                                pe.wait_ge(w_lo, i * 6 + (jj + 1))
                                for k in range(KT):
                                    if jj == 0:
                                        pe.wait_ge(h_split_lo, k + 1)
                                    for pw, px in PASSES:
                                        for c in range(NCH):
                                            last = pe.matmul(ph[jj % 2][:, c, 0:CH], wp[jj % 3][pw][:, k, :], h[px][:, k, c * CH:(c + 1) * CH],
                                                             start=(k == 0 and (pw, px) == PASSES[0]),
                                                             stop=(k == KT - 1 and (pw, px) == PASSES[-1]))
                                last.then_inc(job, 1)
                    pe.wait_ge(tail_ready, 1)
                    pe.transpose(ph[0][0:32, 0, 0:P], tail[:, :], self.ident).then_inc(tail_t, 1)

                @block.scalar
                def _(act):
                    def split(i, jj):
                        act.wait_ge(w_loaded[jj % 3], i * 32 + (jj // 3 * 16 + 16))
                        act.copy(wp[jj % 3][0][:, :, :], w[jj % 3][:, :, :]).then_inc(w_hi, 1)

                    def step(i, last):
                        for jj in range(6):
                            s = jj // 3
                            act.wait_ge(job, i * 6 + (jj + 1))
                            if jj % 3 == 0:
                                act.wait_ge(x_read, i * 2 + (s + 1))
                                act.copy(cb[s][:, :].rearrange("p (c n) -> p c n", n=CH), ph[(3 * s) % 2][:, :, 0:CH]).then_inc(c_read, 1)
                            if jj < 3 or not last:
                                split(i, jj + 3)

                    split(0, 0)
                    for k in range(KT):
                        act.copy(h[0][:, k, :], hT[:, k, :]).then_inc(h_split_hi, 1)
                    split(0, 1)
                    split(0, 2)
                    with act.Fori(0, KT // 2 - 1) as i:
                        step(i, False)
                    step(KT // 2 - 1, True)
                    act.wait_ge(tail_t, 1)
                    act.copy(trow[:, :], ph[0][0:32, 0, 0:P]).then_inc(tail_ev, 1)

                @block.vector
                def _(dve):
                    own = S("cv_dve_link")
                    dve.sem_inc(x_read, 2)
                    dve.sem_inc(b_read, 2)
                    dve.wait_ge(st_t, 1)
                    dve.tensor_copy(wst[:, :], ph[0][:, 0, 0:40]).then_inc(st_ev, 1)
                    dve.wait_ge(st_ev, 1)
                    for s in range(2):
                        dve.memset(u[s][:, :], 0.0).then_inc(own, 1)
                    PER = 14
                    dve.wait_ge(own, 2)

                    def split(i, jj):
                        dve.wait_ge(w_hi, i * 6 + (jj + 1))
                        dve.tensor_tensor(wp[jj % 3][1][:, :, :], w[jj % 3][:, :, :], wp[jj % 3][0][:, :, :].bitcast(F32),
                                          ALU.subtract).then_inc(w_lo, 1)

                    split(0, 0)
                    for k in range(KT):
                        dve.wait_ge(h_split_hi, k + 1)
                        dve.tensor_tensor(h[1][:, k, :], hT[:, k, :], h[0][:, k, :].bitcast(F32), ALU.subtract).then_inc(h_split_lo, 1)
                    split(0, 1)
                    split(0, 2)

                    def step(i, last_step):
                        count = [2]

                        def link(ins):
                            count[0] += 1
                            ins.then_inc(own, 1)
                            dve.wait_ge(own, i * PER + count[0])

                        for s in range(2):
                            m = i * 2 + s
                            if s == 0 or not last_step:
                                split(i, 3 * s + 3)
                            link(dve.tensor_copy(u[s][:, SEQ + 2:SEQ + 4],
                                                 wst[:, 24:40].rearrange("p (j k) -> p j k", k=KT)[:, :, bass.ds(m, 1)].rearrange("p j k -> p (j k)")))
                            dve.wait_ge(job, i * 6 + (3 * s + 2))
                            dve.wait_ge(c_read, i * 2 + (s + 1))
                            for at, pv, a, b in pieces((3 * s + 1) % 2):
                                last = dve.tensor_tensor(cut(u[s][:, at + 2:at + 2 + b - a], b - a), cut(cb[s][:, a:b], b - a), pv, ALU.mult)
                            last.then_inc(x_read, 1)
                            dve.wait_ge(x_read, i * 2 + (s + 3))
                            if s == 0 or not last_step:
                                split(i, 3 * s + 4)
                            n = LEN - 2
                            link(dve.tensor_scalar(acc[:, :], u[s][:, 0:n], wst[:, bass.ds(m, 1)], None, ALU.mult))
                            link(dve.scalar_tensor_tensor(acc[:, :], u[s][:, 1:1 + n], wst[:, bass.ds(m + 8, 1)], acc[:, :], ALU.mult, ALU.add))
                            link(dve.scalar_tensor_tensor(acc[:, :], u[s][:, 2:2 + n], wst[:, bass.ds(m + 16, 1)], acc[:, :], ALU.mult, ALU.add))
                            for g, at in enumerate((SEQ, SEQ + DEC + 2)):
                                link(dve.tensor_copy(tail[:, g * 16:g * 16 + 16].rearrange("p (j k) -> p j k", k=KT)[:, :, bass.ds(m, 1)].rearrange("p j k -> p (j k)"),
                                                u[s][:, at:at + 2]))
                            dve.wait_ge(job, i * 6 + (3 * s + 3))
                            for at, pv, a, b in pieces((3 * s + 2) % 2):
                                dst = cT[:, :, a:b][:, bass.ds(m, 1), :].rearrange("p k n -> p (k n)")
                                last = dve.tensor_tensor(cut(dst, b - a), cut(acc[:, at:at + b - a], b - a), pv, ALU.mult)
                            last.then_inc(b_read, 1)
                            dve.wait_ge(b_read, i * 2 + (s + 3))
                            if s == 0 or not last_step:
                                split(i, 3 * s + 5)
                            link(dve.tensor_copy(acc[:, 0:2], u[s][:, 0:2]))
                        assert count[0] - 2 == PER, count

                    with dve.Fori(0, KT // 2 - 1) as i:
                        step(i, False)
                    step(KT // 2 - 1, True)
                    dve.engine_nop()
                    dve.sem_inc(tail_ready, 1)

    def merge(self):
        nc, I = self.nc, self.I
        S = self.sem
        gate_loaded, out_loaded = S("mg_gate_w"), S("mg_out_w")
        job, s1, s2, y1, y2, merged = map(S, ("mg_job", "mg_sig_conv", "mg_sig_attn", "mg_y_conv", "mg_y_attn", "mg_merged"))
        srcs = ((I["w_in"][0], C_GC), (I["w_conv_out"][0], 0), (I["w_in"][0], C_GA), (I["w_attn_o"][0], 0))
        w_hi, w_lo = S("mg_w_hi"), S("mg_w_lo")
        self.mix_bc = self.cT[:, 0:6, 0:D].rearrange("p (g v) n -> p g v n", g=2)
        self.mix_x = self.cT[:, 6:8, 0:D]
        self.mix_bc_loaded, self.mix_w_loaded, self.mix_x_loaded = S("mx_bc"), S("mx_w"), [S("mx_x0"), S("mx_x1")]
        flat = self.mod_rows.rearrange("r p -> (r p)")
        h, cT, oT = (self.h_hi, self.h_lo), self.cT, self.oT
        PASSES = ((0, 0), (0, 1), (1, 0))
        mT = self.mT
        with ExitStack() as st:
            sb = lambda n, s, d=F32: st.enter_context(nc.sbuf_tensor(n, s, d))
            ps = lambda n, s, d=F32: st.enter_context(nc.psum_tensor(n, s, d))
            wg = sb("mg_gate_wb", [P, KT, P])
            wo = sb("mg_out_wb", [P, KT, P])
            wp = [sb(f"mg_gate_w_{n}", [P, KT, P], F32R) for n in ("hi", "lo")]
            t1 = sb("mg_t1", [P, NCH, CH])
            t2 = sb("mg_t2", [P, NCH, CH])
            ph = [ps(f"mg_ph{i}", [P, 4, 512]) for i in range(2)]
            moving = (None, cT, None, oT)
            with nc.Block() as block:
                @block.sync
                def _(sp):
                    def load(x, i, on=0):
                        src, at = srcs[x]
                        cols = bass.ds(i * P + (at + on * P), P)
                        dst, sem = ((wg, gate_loaded), (wo, out_loaded))[x % 2]
                        sp.dma_start(dst[:, :, :], src[:, cols].rearrange("(k p) n -> p k n", p=P)).then_inc(sem, 16)

                    load(0, 0)
                    load(1, 0)
                    sp.wait_ge(w_lo, 1)
                    load(2, 0)
                    with sp.Fori(0, KT - 1) as i:
                        sp.wait_ge(w_lo, i * 2 + 2)
                        load(0, i + 1)
                        sp.wait_ge(job, i * 4 + 2)
                        load(3, i)
                        sp.wait_ge(job, i * 4 + 4)
                        load(1, i, 1)
                        sp.wait_ge(w_lo, i * 2 + 3)
                        load(2, i + 1)
                    sp.wait_ge(job, KT * 4 - 2)
                    load(3, KT - 1)
                    for g in range(2):
                        for n, v in enumerate((G1, SH2, SC2)):
                            at = (g * 48 + v * 8) * P
                            sp.dma_start(self.mix_bc[:, g, n, :], flat[at:at + D].partition_broadcast(P)).then_inc(self.mix_bc_loaded, 16)
                    for t in range(2):
                        sp.dma_start(self.mix_x[:, t, :], self.x_rows(t)).then_inc(self.mix_x_loaded[t], 16)
                    sp.wait_ge(job, KT * 4 - 1)
                    sp.dma_start(self.mix_w[:, :, 0:D], I["w_mix_out"][0].rearrange("(k p) n -> p k n", p=P)).then_inc(self.mix_w_loaded, 16)

                @block.tensor
                def _(pe):
                    with pe.Fori(0, KT) as i:
                        before = ((s2, 1), (y2, 1), (s1, 1), (y1, 1))
                        for x in range(4):
                            pe.wait_ge(before[x][0], i + before[x][1])
                            if x % 2:
                                pe.wait_ge(out_loaded, i * 32 + (x // 2 * 16 + 16))
                                for k in range(KT):
                                    for c in range(NCH):
                                        last = pe.matmul(ph[1][:, c, 0:CH], wo[:, k, :], moving[x][:, k, c * CH:(c + 1) * CH],
                                                         start=(k == 0), stop=(k == KT - 1))
                            else:
                                pe.wait_ge(w_lo, i * 2 + (x // 2 + 1))
                                for k in range(KT):
                                    for pw, px in PASSES:
                                        for c in range(NCH):
                                            last = pe.matmul(ph[0][:, c, 0:CH], wp[pw][:, k, :], h[px][:, k, c * CH:(c + 1) * CH],
                                                             start=(k == 0 and (pw, px) == PASSES[0]),
                                                             stop=(k == KT - 1 and (pw, px) == PASSES[-1]))
                            last.then_inc(job, 1)

                @block.scalar
                def _(act):
                    def split(i, g):
                        act.wait_ge(gate_loaded, i * 32 + (g * 16 + 16))
                        act.copy(wp[0][:, :, :], wg[:, :, :]).then_inc(w_hi, 1)

                    def step(i, last):
                        act.wait_ge(job, i * 4 + 1)
                        act.wait_ge(merged, i + 1)
                        act.activation(t1[:, :, :], ph[0][:, :, 0:CH], ACT.Sigmoid).then_inc(s1, 1)
                        split(i, 1)
                        act.wait_ge(job, i * 4 + 3)
                        act.activation(t2[:, :, :], ph[0][:, :, 0:CH], ACT.Sigmoid).then_inc(s2, 1)
                        if not last:
                            split(i + 1, 0)

                    act.sem_inc(s2, 1)
                    split(0, 0)
                    with act.Fori(0, KT - 1) as i:
                        step(i, False)
                    step(KT - 1, True)

                @block.vector
                def _(dve):
                    def split(i, g):
                        dve.wait_ge(w_hi, i * 2 + (g + 1))
                        dve.tensor_tensor(wp[1][:, :, :], wg[:, :, :], wp[0][:, :, :].bitcast(F32),
                                          ALU.subtract).then_inc(w_lo, 1)

                    def step(i, last):
                        split(i, 1)
                        dve.wait_ge(job, i * 4 + 2)
                        dve.wait_ge(s1, i + 1)
                        dve.tensor_tensor(t1[:, :, :], t1[:, :, :], ph[1][:, :, 0:CH], ALU.mult).then_inc(y1, 1)
                        if not last:
                            split(i + 1, 0)
                        dve.wait_ge(job, i * 4 + 4)
                        dve.wait_ge(s2, i + 2)
                        dve.tensor_tensor(t2[:, :, :], t2[:, :, :], ph[1][:, :, 0:CH], ALU.mult).then_inc(y2, 1)
                        dve.wait_ge(y1, i + 1)
                        dve.wait_ge(y2, i + 2)
                        dst = mT[:, bass.ds(i, 1), :].rearrange("p k (c n) -> p (k c) n", n=CH)
                        dve.tensor_tensor(dst, t1[:, :, :], t2[:, :, :], ALU.add).then_inc(merged, 1)

                    dve.sem_inc(merged, 1)
                    dve.sem_inc(y2, 1)
                    split(0, 0)
                    with dve.Fori(0, KT - 1) as i:
                        step(i, False)
                    step(KT - 1, True)

    def mix(self):
        nc, I = self.nc, self.I
        S = self.sem
        w_loaded, bc_loaded, x_loaded = self.mix_w_loaded, self.mix_bc_loaded, self.mix_x_loaded
        wr_loaded, mixed, x2_done, sq, ms, rt, h2_ready, h2_stored, t_done, t_ev, lg, sig = map(
            S, ("mx_wr", "mx_mixed", "mx_x2", "mx_sq", "mx_ms", "mx_root", "mx_h2", "mx_stored", "mx_t",
                "mx_t_ev", "mx_logits", "mx_sig"))
        mT, h2T, x2, score = self.mT, self.h2T, self.x2, self.score
        with ExitStack() as st:
            sb = lambda n, s, d=F32: st.enter_context(nc.sbuf_tensor(n, s, d))
            ps = lambda n, s, d=F32: st.enter_context(nc.psum_tensor(n, s, d))
            w = self.mix_w[:, :, 0:D]
            wr = sb("wr", [P, KT, NE])
            bc, x = self.mix_bc, self.mix_x
            h2 = sb("mx_h2b", [P, 2, D])
            junk = sb("mx_junk", [P, D])
            ss, m, r, ri = (sb(f"mx_{n}", [P, NT]) for n in ("ss", "m", "r", "ri"))
            pm = [ps(f"mx_pm{i}", [P, 2, 512]) for i in range(2)]
            pt = ps("mx_pt", [P, 2, 512])
            pl = [ps(f"mx_pl{i}", [P, 512])[:, 0:NE] for i in range(2)]
            with nc.Block() as block:
                @block.sync
                def _(sp):
                    sp.dma_start(wr[:, :, :], I["w_router"][0].rearrange("(k p) n -> p k n", p=P)).then_inc(wr_loaded, 16)
                    for t in range(NT):
                        R = rows_of(t)
                        if t >= 2:
                            sp.wait_ge(x2_done, t - 1)
                            sp.dma_start(x[:R, t % 2, :], self.x_rows(t)).then_inc(x_loaded[t % 2], 16)
                        if t:
                            self.store_h2(sp, t - 1, h2, h2_ready, h2_stored)
                    self.store_h2(sp, NT - 1, h2, h2_ready, h2_stored)
                    sp.wait_ge(h2_stored, 16 * NT)

                @block.tensor
                def _(pe):
                    def trans(t):
                        R = rows_of(t)
                        pe.wait_ge(h2_ready, t + 1)
                        if t:
                            pe.wait_ge(t_ev, t)
                        for k in range(KT):
                            last = pe.transpose(pt[:, k // 4, (k % 4) * P:(k % 4) * P + R],
                                                h2[:R, t % 2, k * P:(k + 1) * P], self.ident[:R, :R])
                        last.then_inc(t_done, 1)

                    def logits(t):
                        R = rows_of(t)
                        pe.wait_ge(t_ev, t + 1)
                        pe.wait_ge(wr_loaded, 16)
                        if t >= 2:
                            pe.wait_ge(sig, t - 1)
                        for k in range(KT):
                            last = pe.matmul(pl[t % 2][:R, :], h2T[:, k, t * P:t * P + R], wr[:, k, :],
                                             start=(k == 0), stop=(k == KT - 1))
                        last.then_inc(lg, 1)

                    pe.wait_ge(w_loaded, 16)
                    for t in range(NT):
                        R = rows_of(t)
                        if t >= 2:
                            pe.wait_ge(x2_done, t - 1)
                        for k in range(KT):
                            for h in range(2):
                                last = pe.matmul(pm[t % 2][:R, h, :], mT[:, k, t * P:t * P + R], w[:, k, h * 512:(h + 1) * 512],
                                                 start=(k == 0), stop=(k == KT - 1))
                        last.then_inc(mixed, 1)
                        if t:
                            trans(t - 1)
                        if t >= 2:
                            logits(t - 2)
                    trans(NT - 1)
                    logits(NT - 2)
                    logits(NT - 1)

                @block.scalar
                def _(act):
                    link = self.link_of(act, "act")

                    def evac(t):
                        R = rows_of(t)
                        act.wait_ge(t_done, t + 1)
                        for h in range(2):
                            last = act.copy(h2T[:, 4 * h:4 * h + 4, t * P:t * P + R],
                                            pt[:, h, :].rearrange("p (k n) -> p k n", n=P)[:, :, 0:R])
                        last.then_inc(t_ev, 1)

                    def sigmoid(t):
                        R = rows_of(t)
                        act.wait_ge(lg, t + 1)
                        act.activation(score[:R, t, :], pl[t % 2][:R, :], ACT.Sigmoid).then_inc(sig, 1)

                    for t in range(NT):
                        R = rows_of(t)
                        act.wait_ge(x2_done, t + 1)
                        link(act.activation(junk[:R, :], x2[:R, t, :], ACT.Square, accum_out=ss[:R, t:t + 1]))
                        act.sem_inc(sq, 1)
                        act.wait_ge(ms, t + 1)
                        act.activation(r[:R, t:t + 1], m[:R, t:t + 1], ACT.Sqrt).then_inc(rt, 1)
                        if t:
                            evac(t - 1)
                        if t >= 2:
                            sigmoid(t - 2)
                    evac(NT - 1)
                    sigmoid(NT - 2)
                    sigmoid(NT - 1)

                @block.vector
                def _(dve):
                    link = self.link_of(dve, "dve")
                    dve.memset(score[CHUNK:P, NT - 1, :], 0.5)
                    dve.wait_ge(bc_loaded, 96)
                    for t in range(NT):
                        R = rows_of(t)
                        g = int(t == NT - 1)
                        dve.wait_ge(mixed, t + 1)
                        dve.wait_ge(x_loaded[t % 2], 16 * (t // 2 + 1))
                        link(dve.tensor_tensor(x2[:R, t, :].rearrange("p (a n) -> p a n", a=2), pm[t % 2][:R, :, :],
                                               bc[:R, g, 0, :].rearrange("p (a n) -> p a n", a=2), ALU.mult))
                        dve.tensor_tensor(x2[:R, t, :], x2[:R, t, :], x[:R, t % 2, :], ALU.add).then_inc(x2_done, 1)
                        dve.wait_ge(sq, t + 1)
                        dve.tensor_scalar(m[:R, t:t + 1], ss[:R, t:t + 1], 1.0 / D, EPS, ALU.mult, ALU.add).then_inc(ms, 1)
                        dve.wait_ge(rt, t + 1)
                        link(dve.reciprocal(ri[:R, t:t + 1], r[:R, t:t + 1]))
                        if t >= 2:
                            dve.wait_ge(h2_stored, 16 * (t - 1))
                            dve.wait_ge(t_done, t - 1)
                        link(dve.scalar_tensor_tensor(h2[:R, t % 2, :], x2[:R, t, :], ri[:R, t:t + 1], bc[:R, g, 2, :], ALU.mult, ALU.mult))
                        dve.tensor_tensor(h2[:R, t % 2, :], h2[:R, t % 2, :], bc[:R, g, 1, :], ALU.add).then_inc(h2_ready, 1)

    def store_h2(self, sp, t, h2, h2_ready, h2_stored):
        R = rows_of(t)
        sp.wait_ge(h2_ready, t + 1)
        sp.dma_start(self.h2_rows[t * P:t * P + R, :], h2[:R, t % 2, :]).then_inc(h2_stored, 16)

    def routing_and_shared(self):
        nc, I = self.nc, self.I
        S = self.sem
        con, score = self.con, self.score
        place_w, place_x = self.place_w, self.place_x
        zeroed = S("rt_zeroed")
        bias_l, mask_ready, ranked, counted, nblk_ready, start_done, cmp_ready, eb_done, hot, hot_used, tab = map(
            S, ("rt_bias", "rt_mask", "rt_ranked", "rt_counted", "rt_nblk", "rt_start", "rt_cmp",
                "rt_eb", "rt_hot", "rt_hot_used", "rt_table"))
        wl, w_down_l, bl, gate_up, gate_out, up_out, silu, ready, down, y_out, gated, added = map(
            S, ("sh_w", "sh_w_down", "sh_bc", "sh_gate_up", "sh_gate_out", "sh_up_out", "sh_silu", "sh_ready", "sh_down",
                "sh_y_out", "sh_gated", "sh_added"))
        h2T, x2 = self.h2T, self.x2
        flat = self.mod_rows.rearrange("r p -> (r p)")
        NF = DSH // P
        units = [(f, cp) for f in range(NF) for cp in range(2)]
        with ExitStack() as st:
            sb = lambda n, s, d=F32: st.enter_context(nc.sbuf_tensor(n, s, d))
            ps = lambda n, s, d=F32: st.enter_context(nc.psum_tensor(n, s, d))
            bias = sb("rt_biasb", [P, NE])
            biased = sb("biased", [P, NT, NE])
            top = sb("rt_top", [P, NT * NG, 8])
            gsc = sb("gsc", [P, NT, NG])
            cmpg = sb("cmpg", [P, NT * NG, NG])
            eqg = sb("eqg", [P, NT * NG, NG])
            grank = sb("grank", [P, NT * NG])
            gmask = sb("gmask", [P, NT * NG])
            gneg = sb("gneg", [P, NT * NG])
            masked = sb("rt_masked", [P, NT, NE])
            best = sb("best", [P, NT, 8])
            rep = sb("rep", [P, NT, NE])
            mask = sb("mask", [P, NT, NE])
            maskh = sb("maskh", [P, NT, NE], BF16)
            trih = sb("trih", [P, P], BF16)
            oneh = sb("oneh", [P, P], BF16)
            wd = sb("wd", [P, NT, NE])
            wsum = sb("wsum", [P, NT])
            rsum = sb("rsum", [P, NT])
            cnt = sb("cnt", [NE, 1])
            over = sb("over", [NE, NTHR])
            nblk = sb("nblk", [NE, 1])
            nblkh = sb("nblkh", [NE, P], BF16)
            nzh = sb("nzh", [NE, 1], BF16)
            enzh = sb("enzh", [NE, 1], BF16)
            nz = sb("nz", [NE, 1])
            ordc = sb("ordc", [NE, 1])
            ohw = sb("ohw", [NE, NE], BF16)
            ordf = sb("ordf", [1, NBP])
            chg = sb("chg", [1, NBP])
            usedf = sb("usedf", [1, 1])
            startc = sb("startc", [NE, 1])
            startr = sb("startr", [P, NE])
            cmpb = sb("cmpb", [NE, NBP], BF16)
            key = sb("key", [P, NT, NE])
            key8 = sb("key8", [P, NT, 8])
            eq8 = sb("eq8", [P, 8, NE])
            slot = sb("slot", [P, NT * 8])
            sloti = sb("sloti", [P, NT * 8], I32)
            lo = sb("lo", [P, NT * 8], I32)
            hi = sb("hi", [P, NT * 8], I32)
            lof = sb("lof", [P, NT * 8])
            hif = sb("hif", [P, NT * 8])
            w8 = sb("w8", [P, NT, TOPK])
            hp = sb("hot_p", [P, 4, P])
            hc = sb("hot_c", [P, 4, 2, NCOL])
            zero = sb("rt_zero", [P, D])
            tabf = sb("tabf", [P, NCOL])
            miss = sb("miss", [P, NCOL])
            pr = [ps(f"rt_pr{i}", [P, 8, NE]) for i in range(2)]
            small = ps("rt_small", [P, 512])
            psr = small[:, 0:NE]
            psc = small[0:NE, NE:NE + 2]
            pst = small[:, NE + 2:NE + 4]
            pc = small[0:NE, NE + 4:NE + 5]
            ord_at, exp_at = 128, 128 + NBP
            ptb = ps("rt_ptb", [P, 512])[:, 0:2 * NCOL].rearrange("p (a n) -> p a n", a=2)
            rank = lambda t: pr[t // 8][:, t % 8, :]
            g2b = sb("sh_g2b", [P, 2, D])
            wg = sb("sh_wg", [P, KT, DSH])
            wu = sb("sh_wu", [P, KT, DSH])
            wdn = sb("sh_wd", [P, NF, D])
            s_, g_, u_ = (sb(f"sh_{n}", [P, 2, CH]) for n in ("s", "g", "u"))
            a_ = sb("sh_ab", [P, NF, TOK])
            tmp = sb("sh_tmp", [P, 2, D])
            ph = [ps(f"sh_ph{i}", [P, 2, 512]) for i in range(2)]
            with nc.Block() as block:
                @block.sync
                def _(sp):
                    sp.dma_start(bias[:, :], I["router_bias"][0].partition_broadcast(P)).then_inc(bias_l, 16)
                    sp.dma_start(wg[:, :, :], I["w_sh_gate"][0].rearrange("(k p) n -> p k n", p=P)).then_inc(wl, 16)
                    sp.dma_start(wu[:, :, :], I["w_sh_up"][0].rearrange("(k p) n -> p k n", p=P)).then_inc(wl, 16)
                    sp.dma_start(wdn[:, :, :], I["w_sh_down"][0].rearrange("(k p) n -> p k n", p=P)).then_inc(w_down_l, 16)
                    for g in range(2):
                        at = (g * 48 + G2 * 8) * P
                        sp.dma_start(g2b[:, g, :], flat[at:at + D].partition_broadcast(P)).then_inc(bl, 16)
                    sp.wait_ge(zeroed, 1)
                    for t in range(NT):
                        sp.dma_start(self.sum_rows[t * P:t * P + rows_of(t), :], zero[:rows_of(t), :]).then_inc(self.sum_cleared, 16)

                @block.vector
                def _(dve):
                    link = self.link_of(dve, "dve")
                    link(dve.tensor_copy(trih[:, :], con[:, C_TRI:C_TRI + P]))
                    link(dve.memset(oneh[:, :], 1.0))
                    dve.memset(zero[:, :], 0.0).then_inc(zeroed, 1)
                    dve.wait_ge(bias_l, 16)
                    link(dve.tensor_tensor(biased[:, :, :], score[:, :, :],
                                           bias[:, :].unsqueeze(1).to_broadcast([P, NT, NE]), ALU.add))
                    for t in range(NT):
                        for g in range(NG):
                            last = dve.max(top[:, t * NG + g, :], biased[:, t, g * GS:(g + 1) * GS])
                    link(last)
                    gs2 = gsc[:, :, :].rearrange("p t g -> p (t g)")
                    link(dve.tensor_tensor(gs2, top[:, :, 0], top[:, :, 1], ALU.add))
                    for t in range(NT):
                        a = gsc[:, t, :].unsqueeze(1).to_broadcast([P, NG, NG])
                        b = gsc[:, t, :].unsqueeze(2).to_broadcast([P, NG, NG])
                        dve.tensor_tensor(cmpg[:, t * NG:(t + 1) * NG, :], a, b, ALU.is_gt)
                        last = dve.tensor_tensor(eqg[:, t * NG:(t + 1) * NG, :], a, b, ALU.is_equal)
                    link(last)
                    low = con[:, C_LOW:C_LOW + NG * NG].rearrange("p (g h) -> p g h", h=NG)
                    for t in range(NT):
                        v = eqg[:, t * NG:(t + 1) * NG, :]
                        last = dve.tensor_tensor(v, v, low, ALU.mult)
                    link(last)
                    link(dve.tensor_tensor(cmpg[:, :, :], cmpg[:, :, :], eqg[:, :, :], ALU.add))
                    link(dve.tensor_reduce(grank[:, :], cmpg[:, :, :], AX.X, ALU.add))
                    link(dve.tensor_scalar(gmask[:, :], grank[:, :], float(TOPG), None, ALU.is_lt))
                    link(dve.tensor_scalar(gneg[:, :], gmask[:, :], -1.0, 1e30, ALU.add, ALU.mult))
                    m3 = masked[:, :, :].rearrange("p t (g e) -> p (t g) e", e=GS)
                    b3 = biased[:, :, :].rearrange("p t (g e) -> p (t g) e", e=GS)
                    link(dve.tensor_tensor(m3, b3, gmask[:, :].unsqueeze(2).to_broadcast([P, NT * NG, GS]), ALU.mult))
                    link(dve.tensor_tensor(m3, m3, gneg[:, :].unsqueeze(2).to_broadcast([P, NT * NG, GS]), ALU.add))
                    for t in range(NT):
                        last = dve.max(best[:, t, :], masked[:, t, :])
                    link(last)
                    for t in range(NT):
                        last = dve.match_replace(rep[:, t, :], best[:, t, :], masked[:, t, :], -3e38)
                    link(last)
                    link(dve.tensor_tensor(mask[:, :, :], rep[:, :, :], masked[:, :, :], ALU.not_equal))
                    link(dve.tensor_tensor(wd[:, :, :], mask[:, :, :], score[:, :, :], ALU.mult))
                    link(dve.tensor_reduce(wsum[:, :], wd[:, :, :], AX.X, ALU.add))
                    link(dve.reciprocal(rsum[:, :], wsum[:, :]))
                    for t in range(NT):
                        last = dve.tensor_scalar(wd[:, t, :], wd[:, t, :], rsum[:, t:t + 1], ROUTED_SCALE, ALU.mult, ALU.mult)
                    link(last)
                    link(dve.memset(mask[CHUNK:P, NT - 1, :], 0.0))
                    link(dve.tensor_copy(maskh[:, :, :], mask[:, :, :]))
                    dve.sem_inc(mask_ready, 1)
                    dve.wait_ge(counted, 1)
                    link(dve.tensor_copy(cnt[:, :], pc[:, :]))
                    link(dve.tensor_scalar(over[:, :], con[0:NE, C_THR:C_THR + NTHR], cnt[:, 0:1], None, ALU.is_lt))
                    link(dve.tensor_reduce(nblk[:, :], over[:, :], AX.X, ALU.add))
                    link(dve.tensor_scalar(nz[:, :], nblk[:, :], 0.0, None, ALU.is_gt))
                    link(dve.tensor_copy(nzh[:, :], nz[:, :]))
                    link(dve.tensor_tensor(enzh[:, :], nz[:, :], con[0:NE, C_ROW:C_ROW + 1], ALU.mult))
                    dve.tensor_copy(nblkh[:, :], nblk[:, 0:1].to_broadcast([NE, P])).then_inc(nblk_ready, 1)
                    dve.wait_ge(start_done, 1)
                    link(dve.tensor_copy(startr[:, :], psr[:, :]))
                    link(dve.tensor_copy(startc[:, :], psc[:, 0:1]))
                    link(dve.tensor_copy(ordc[:, :], psc[:, 1:2]))
                    link(dve.tensor_copy(self.n_blocks[:, :], pst[0:1, 0:1]))
                    link(dve.tensor_copy(self.n_used[:, :], pst[0:1, 1:2]))
                    link(dve.tensor_copy(usedf[:, :], pst[0:1, 1:2]))
                    link(dve.tensor_scalar(ohw[:, :], con[0:NE, C_IB:C_IB + NE], ordc[:, 0:1], None, ALU.is_equal))
                    dve.tensor_scalar(cmpb[:, :], con[0:NE, C_IB:C_IB + NBP], startc[:, 0:1], None, ALU.is_ge).then_inc(cmp_ready, 1)
                    dve.wait_ge(eb_done, 1)
                    link(dve.tensor_scalar(ordf[:, :], small[0:1, ord_at:ord_at + NBP], -1.0, None, ALU.add))
                    link(dve.tensor_copy(self.ord_e[:, :], small[0:1, exp_at:exp_at + NE]))
                    link(dve.tensor_copy(self.blk_ord[:, :], ordf[:, :]))
                    link(dve.memset(chg[:, :], 1.0))
                    link(dve.tensor_tensor(chg[:, 1:NBP], ordf[:, 1:NBP], ordf[:, 0:NBP - 1], ALU.not_equal))
                    link(dve.tensor_scalar(ordf[:, :], ordf[:, :], 1.0, None, ALU.add))
                    link(dve.scalar_tensor_tensor(chg[:, :], ordf[:, :], usedf[:, 0:1], chg[:, :], ALU.is_lt, ALU.mult))
                    link(dve.tensor_tensor(self.blk_split[:, :], chg[:, :], ordf[:, :], ALU.mult))
                    dve.wait_ge(ranked, 1)
                    for t in range(NT):
                        last = dve.scalar_tensor_tensor(key[:, t, :], startr[:, :], float(BLK), rank(t), ALU.mult, ALU.add)
                    link(last)
                    link(dve.tensor_scalar(key[:, :, :], key[:, :, :], -1.0, KEY0, ALU.mult, ALU.add))
                    link(dve.tensor_tensor(key[:, :, :], key[:, :, :], mask[:, :, :], ALU.mult))
                    for t in range(NT):
                        last = dve.max(key8[:, t, :], key[:, t, :])
                    link(last)
                    link(dve.tensor_scalar(slot[:, :], key8[:, :, :].rearrange("p t j -> p (t j)"), -1.0, KEY0, ALU.mult, ALU.add))
                    link(dve.tensor_copy(sloti[:, :], slot[:, :]))
                    dve.tensor_single_scalar(lo[:, :], sloti[:, :], P - 1, ALU.bitwise_and)
                    link(dve.tensor_single_scalar(hi[:, :], sloti[:, :], 7, ALU.logical_shift_right))
                    dve.tensor_copy(lof[:, :], lo[:, :])
                    link(dve.tensor_copy(hif[:, :], hi[:, :]))
                    for t in range(NT):
                        link(dve.tensor_tensor(eq8[:, :, :], key[:, t, :].unsqueeze(1).to_broadcast([P, 8, NE]),
                                               key8[:, t, :].unsqueeze(2).to_broadcast([P, 8, NE]), ALU.is_equal))
                        link(dve.tensor_tensor(eq8[:, :, :], eq8[:, :, :], wd[:, t, :].unsqueeze(1).to_broadcast([P, 8, NE]), ALU.mult))
                        link(dve.tensor_reduce(w8[:, t, :], eq8[:, :, :], AX.X, ALU.add))
                    for n in range(NT * TOPK):
                        if n >= 4:
                            dve.wait_ge(hot_used, n - 3)
                        dve.tensor_scalar(hp[:, n % 4, :], con[:, C_IP:C_IP + P], lof[:, n:n + 1], None, ALU.is_equal)
                        dve.tensor_scalar(hc[:, n % 4, 0, :], con[:, C_IC:C_IC + NCOL], hif[:, n:n + 1],
                                          con[:, C_VAL + n:C_VAL + n + 1], ALU.is_equal, ALU.mult)
                        dve.tensor_scalar(hc[:, n % 4, 1, :], con[:, C_IC:C_IC + NCOL], hif[:, n:n + 1],
                                          w8[:, n // TOPK, n % TOPK:n % TOPK + 1], ALU.is_equal, ALU.mult).then_inc(hot, 1)
                    dve.wait_ge(tab, 1)
                    link(dve.tensor_copy(tabf[:, :], ptb[:, 0, :]))
                    link(dve.tensor_copy(place_w[:, :], ptb[:, 1, :]))
                    link(dve.tensor_scalar(miss[:, :], tabf[:, :], 0.0, NOWHERE, ALU.is_equal, ALU.mult))
                    link(dve.scalar_tensor_tensor(tabf[:, :], tabf[:, :], -1.0, miss[:, :], ALU.add, ALU.add))
                    link(dve.tensor_scalar(tabf[:, :], tabf[:, :], NOWHERE, None, ALU.min))
                    link(dve.tensor_copy(place_x[:, :], tabf[:, :]))

                @block.scalar
                def _(act):
                    for q, (f, cp) in enumerate(units):
                        act.wait_ge(gate_up, 2 * q + 1)
                        if q:
                            act.wait_ge(ready, q)
                        act.activation(s_[:, :, :], ph[0][:, :, 0:CH], ACT.Sigmoid)
                        act.copy(g_[:, :, :], ph[0][:, :, 0:CH]).then_inc(gate_out, 1)
                        act.wait_ge(gate_up, 2 * q + 2)
                        act.copy(u_[:, :, :], ph[1][:, :, 0:CH]).then_inc(up_out, 1)
                    for t in range(NT):
                        R = rows_of(t)
                        act.wait_ge(down, t + 1)
                        if t >= 2:
                            act.wait_ge(added, t - 1)
                        act.copy(tmp[:R, t % 2, :].rearrange("p (a n) -> p a n", a=2), ph[t % 2][:R, :, :]).then_inc(y_out, 1)

                @block.gpsimd
                def _(pool):
                    for q, (f, cp) in enumerate(units):
                        pool.wait_ge(gate_out, q + 1)
                        pool.tensor_tensor(s_[:, :, :], s_[:, :, :], g_[:, :, :], ALU.mult).then_inc(silu, 1)
                        pool.wait_ge(silu, q + 1)
                        pool.wait_ge(up_out, q + 1)
                        pool.tensor_tensor(a_[:, f, 2 * cp * CH:2 * (cp + 1) * CH].rearrange("p (c n) -> p c n", n=CH),
                                           s_[:, :, :], u_[:, :, :], ALU.mult).then_inc(ready, 1)
                    pool.wait_ge(bl, 32)
                    for t in range(NT):
                        R = rows_of(t)
                        g = int(t == NT - 1)
                        v = tmp[:R, t % 2, :]
                        pool.wait_ge(y_out, t + 1)
                        pool.tensor_tensor(v, v, g2b[:R, g, :], ALU.mult).then_inc(gated, 1)
                        pool.wait_ge(gated, t + 1)
                        pool.tensor_tensor(x2[:R, t, :], x2[:R, t, :], v, ALU.add).then_inc(added, 1)

                @block.tensor
                def _(pe):
                    def unit(q):
                        f, cp = units[q]
                        for half, w in enumerate((wg, wu)):
                            pe.wait_ge(wl, 32)
                            if q:
                                pe.wait_ge((gate_out, up_out)[half], q)
                            for k in range(KT):
                                for c in range(2):
                                    at = (2 * cp + c) * CH
                                    last = pe.matmul(ph[half][:, c, 0:CH], w[:, k, f * P:(f + 1) * P], h2T[:, k, at:at + CH],
                                                     start=(k == 0), stop=(k == KT - 1))
                            last.then_inc(gate_up, 1)

                    def shared_down(t):
                        R = rows_of(t)
                        if t == 0:
                            pe.wait_ge(w_down_l, 16)
                            pe.wait_ge(ready, len(units))
                        if t >= 2:
                            pe.wait_ge(y_out, t - 1)
                        for f in range(NF):
                            for h in range(2):
                                last = pe.matmul(ph[t % 2][:R, h, :], a_[:, f, t * P:t * P + R], wdn[:, f, h * 512:(h + 1) * 512],
                                                 start=(f == 0), stop=(f == NF - 1))
                        last.then_inc(down, 1)

                    unit(0)
                    unit(1)
                    pe.wait_ge(mask_ready, 1)
                    for t in range(NT):
                        last = pe.matmul(pc[:, :], maskh[:, t, :], oneh[:, 0:1], start=(t == 0), stop=(t == NT - 1))
                    last.then_inc(counted, 1)
                    for t in range(NT):
                        last = pe.matmul(rank(t), trih[:, :], maskh[:, t, :], start=True, stop=(t == 0))
                        for b in range(t):
                            last = pe.matmul(rank(t), oneh[:, :], maskh[:, b, :], start=False, stop=(b == t - 1))
                    last.then_inc(ranked, 1)
                    pe.wait_ge(nblk_ready, 1)
                    pe.matmul(psr[:, :], nblkh[:, :], trih[0:NE, 0:NE], start=True, stop=True)
                    pe.matmul(psc[:, 0:1], trih[0:NE, 0:NE], nblkh[:, 0:1], start=True, stop=True)
                    pe.matmul(psc[:, 1:2], trih[0:NE, 0:NE], nzh[:, :], start=True, stop=True)
                    pe.matmul(pst[:, 0:1], oneh[0:NE, :], nblkh[:, 0:1], start=True, stop=True)
                    pe.matmul(pst[:, 1:2], oneh[0:NE, :], nzh[:, :], start=True, stop=True).then_inc(start_done, 1)
                    pe.wait_ge(cmp_ready, 1)
                    pe.matmul(small[0:1, ord_at:ord_at + NBP], nzh[:, :], cmpb[:, :], start=True, stop=True)
                    pe.matmul(small[0:1, exp_at:exp_at + NE], enzh[:, :], ohw[:, :], start=True, stop=True).then_inc(eb_done, 1)
                    unit(2)
                    unit(3)
                    for n in range(NT * TOPK):
                        if n % TOPK == 0:
                            shared_down(n // TOPK)
                        pe.wait_ge(hot, n + 1)
                        pe.matmul(ptb[:, :, :], hp[:, n % 4, :], hc[:, n % 4, :, :], start=(n == 0), stop=(n == NT * TOPK - 1)).then_inc(hot_used, 1)
                    pe.wait_ge(hot_used, NT * TOPK)
                    pe.sem_inc(tab, 1)

    def experts(self):
        nc, I = self.nc, self.I
        S = self.sem
        NF = DE // P
        w_loaded = [S(f"ex_w{i}") for i in range(3)]
        rows_gathered, y_stored = S("ex_rows_gathered"), S("ex_y_stored")
        sp_turn = S("ex_sp_turn")
        idx, turn, y_free = S("ex_index"), S("ex_turn"), S("ex_y_free")
        transposed = S("ex_transposed")
        x_hi, x_lo = S("ex_x_hi"), S("ex_x_lo")
        w_hi, w_lo = S("ex_w_hi"), S("ex_w_lo")
        AHEAD = 12
        gate_up, h_transposed = S("ex_gate_up"), S("ex_h_transposed")
        down = S("ex_down")
        sig_done, silu_done, hidden = S("ex_sigmoid"), S("ex_silu"), S("ex_hidden")
        h_hi, h_lo = S("ex_h_hi"), S("ex_h_lo")
        y_ready = S("ex_y_ready")
        srcs = (I["w_exp_gate"][0], I["w_exp_up"][0], I["w_exp_down"][0])
        place_x, place_w = self.place_x, self.place_w
        with ExitStack() as st:
            sb = lambda n, s, d=F32: st.enter_context(nc.sbuf_tensor(n, s, d))
            ps = lambda n, s, d=F32: st.enter_context(nc.psum_tensor(n, s, d))
            PIECE = KT * DE
            stage = [sb(f"ex_stage{i}", [P, 2 if i < 2 else 1, PIECE]) for i in range(3)]
            wgu = [sb(f"ex_wgu_{n}", [P, 2, KT, 2 * DE], F32R) for n in ("hi", "lo")]
            wdn = [sb(f"ex_wdn_{n}", [P, 2, NF * D], F32R) for n in ("hi", "lo")]
            xr = sb("ex_rows", [P, D])
            ixx = sb("ex_index_gather", [P, 1], I32)
            ixy = sb("ex_index_scatter", [P, 1], I32)
            wcol = sb("ex_place_weights", [P, 1])
            xT = [sb(f"ex_xT_{n}", [P, KT, P], F32R) for n in ("hi", "lo")]
            s_ = sb("ex_s", [P, DE])
            h = sb("ex_h", [P, DE])
            hT = [sb(f"ex_hT_{n}", [P, NF, P], F32R) for n in ("hi", "lo")]
            y = sb("ex_y", [P, 2, 512])
            pt = [ps(f"ex_pt{i}", [P, 4, P]) for i in range(2)]
            pgu = ps("ex_pgu", [P, 2 * DE])
            py = [ps(f"ex_py{j}", [P, 512]) for j in range(2)]
            ph = ps("ex_ph", [P, 512])[:, 0:NF * P].rearrange("p (f n) -> p f n", f=NF)
            PASSES = ((0, 0), (0, 1), (1, 0))

            def blocks_of(eng):
                return eng.value_load(self.n_blocks[0:1, 0:1], min_val=TOPK, max_val=MAX_BLOCKS)

            def table(eng, t, at, top):
                return eng.value_load(t[0:1, bass.ds(at, 1)], min_val=0, max_val=top)

            with nc.Block() as block:
                @block.sync
                def _(sp):
                    n = sp.value_load(self.n_used[0:1, 0:1], min_val=TOPK, max_val=NE)

                    def expert(w):
                        return table(sp, self.ord_e, w, NE - 1)

                    def load(p, e, slot):
                        k = KT if p < 2 else NF
                        sp.dma_start(stage[p][:, bass.ds(slot, 1), :].rearrange("p s (k n) -> p (s k) n", k=k),
                                     srcs[p][bass.ds(e, 1)].rearrange("e (k p) n -> p (e k) n", p=P)).then_inc(w_loaded[p], 16)

                    def wait(sem, value):
                        sp.wait_ge(sem, value)
                        sp.sem_inc(sp_turn, 1)

                    e, following = expert(0), expert(1)
                    for p in range(3):
                        load(p, e, 0)
                    for p in range(2):
                        sp.wait_ge(w_loaded[p], 16)
                        load(p, following, 1)
                    with sp.Fori(0, n - 2) as i:
                        e, following = expert(i + 1), expert(i + 2)
                        for p in range(2):
                            wait(w_lo, i * 6 + (2 * (p + 1) + AHEAD))
                            wait(w_loaded[p], i * 16 + 32)
                            load(p, following, i % 2)
                        wait(w_lo, i * 6 + (6 + AHEAD))
                        load(2, e, 0)
                    with sp.Fori(n - 2, n - 1) as i:
                        e = expert(i + 1)
                        wait(w_lo, i * 6 + (6 + AHEAD))
                        load(2, e, 0)

                @block.gpsimd
                def _(pool):
                    n = blocks_of(pool)

                    def gather():
                        pool.indirect_dma_start(xr[:, :], None, self.h2_rows, bass.IndirectOffsetOnAxis(ap=ixx[:, 0:1], axis=0),
                                                bounds_check=TOK - 1, oob_is_err=False).then_inc(rows_gathered, 16)

                    def wait(sem, value):
                        pool.wait_ge(sem, value)
                        pool.sem_inc(turn, 1)

                    pool.dma_start(xr[:, :], self.h2_rows[0:P, :]).then_inc(y_stored, 16)
                    pool.tensor_copy(ixx[:, :], place_x[:, 0:1]).then_inc(idx, 1)
                    pool.wait_ge(idx, 1)
                    pool.wait_ge(y_stored, 16)
                    gather()
                    for b in (1, 2):
                        pool.wait_ge(transposed, 2 * b)
                        pool.tensor_copy(ixx[:, :], place_x[:, b:b + 1]).then_inc(idx, 1)
                        pool.wait_ge(idx, b + 1)
                        gather()
                    pool.wait_ge(self.sum_cleared, 16 * NT)

                    def scatter(b, count):
                        wait(y_stored, b * 16 + 16)
                        pool.tensor_copy(wcol[:, :], place_w[:, bass.ds(b, 1)]).then_inc(y_free, 1)
                        pool.tensor_copy(ixy[:, :], place_x[:, bass.ds(b, 1)]).then_inc(idx, 1)
                        wait(idx, count)
                        wait(y_ready, b * 2 + 6)
                        pool.indirect_dma_start(self.sum_rows, bass.IndirectOffsetOnAxis(ap=ixy[:, 0:1], axis=0),
                                                y[:, :, :].rearrange("p a n -> p (a n)"), None,
                                                bounds_check=TOK - 1, oob_is_err=False,
                                                compute_op=ALU.add).then_inc(y_stored, 16)

                    with pool.Fori(0, n - 1) as i:
                        wait(transposed, i * 2 + 6)
                        pool.tensor_copy(ixx[:, :], place_x[:, bass.ds(i + 3, 1)]).then_inc(idx, 1)
                        wait(idx, i * 2 + 4)
                        gather()
                        scatter(i, i * 2 + 5)
                    scatter(n - 1, n * 2 + 2)
                    wait(rows_gathered, n * 16 + 32)
                    wait(y_stored, n * 16 + 16)

                @block.tensor
                def _(pe):
                    n = blocks_of(pe)

                    def rows(b, lo_value):
                        pe.wait_ge(rows_gathered, b * 16 + 16)
                        for r in range(2):
                            if lo_value is not None:
                                pe.wait_ge(x_lo, lo_value + r)
                            for k in range(4):
                                last = pe.transpose(pt[r][:, k, :], xr[:, (4 * r + k) * P:(4 * r + k + 1) * P], self.ident)
                            last.then_inc(transposed, 1)

                    def gates(b, ordinal, slot):
                        pe.wait_ge(x_lo, b * 2 + 2)
                        pe.wait_ge(w_lo, ordinal * 6 + (4 + AHEAD))
                        for k in range(KT):
                            for a, c in PASSES:
                                w = wgu[c][:, bass.ds(slot, 1), k, :].rearrange("p s n -> p (s n)")
                                last = pe.matmul(pgu[:, :], xT[a][:, k, :], w, start=(k == 0 and (a, c) == PASSES[0]),
                                                 stop=(k == KT - 1 and (a, c) == PASSES[-1]))
                        last.then_inc(gate_up, 1)

                    def hiddens(b):
                        pe.wait_ge(hidden, b + 1)
                        for f in range(NF):
                            last = pe.transpose(ph[:, f, :], h[:, f * P:(f + 1) * P], self.ident)
                        last.then_inc(h_transposed, 1)

                    def downs(b, ordinal):
                        slot = ordinal % 2
                        pe.wait_ge(h_lo, b + 1)
                        pe.wait_ge(w_lo, ordinal * 6 + (6 + AHEAD))
                        for j in range(2):
                            pe.wait_ge(y_ready, b * 2 + (j + 3))
                            for f in range(NF):
                                for a, c in PASSES:
                                    w = wdn[c][:, bass.ds(slot, 1), f * D + j * 512:f * D + (j + 1) * 512].rearrange("p s n -> p (s n)")
                                    last = pe.matmul(py[j][:, :], hT[a][:, f, :], w, start=(f == 0 and (a, c) == PASSES[0]),
                                                     stop=(f == NF - 1 and (a, c) == PASSES[-1]))
                            last.then_inc(down, 1)

                    pe.sem_inc(y_ready, 4)
                    pe.sem_inc(down, 2)
                    rows(0, None)
                    gates(0, 0, 0)
                    rows(1, 1)
                    hiddens(0)
                    before = pe.alloc_register("ordinal_of_block_before")
                    pe.reg_mov(before, 0)
                    with pe.Fori(0, n - 1) as i:
                        ordinal = table(pe, self.blk_ord, i + 1, NE - 1)
                        gates(i + 1, ordinal, ordinal % 2)
                        rows(i + 2, i * 2 + 3)
                        downs(i, pe.snap(before, min_val=0, max_val=NE - 1))
                        pe.reg_mov(before, ordinal)
                        hiddens(i + 1)
                    downs(n - 1, pe.snap(before, min_val=0, max_val=NE - 1))

                def halves(part, slot, p):
                    for q in range(2):
                        if p < 2:
                            k = slice(q * KT // 2, (q + 1) * KT // 2)
                            yield wgu[part][:, bass.ds(slot, 1), k, p * DE:(p + 1) * DE].rearrange("p s k n -> p (s k) n"), \
                                stage[p][:, bass.ds(slot, 1), :].rearrange("p s (k n) -> p (s k) n", k=KT)[:, k, :]
                        else:
                            n = slice(q * PIECE // 2, (q + 1) * PIECE // 2)
                            yield wdn[part][:, bass.ds(slot, 1), n].rearrange("p s n -> p (s n)"), stage[2][:, 0, n]

                @block.scalar
                def _(act):
                    n = blocks_of(act)

                    def split(ordinal, slot, which):
                        for p in which:
                            act.wait_ge(w_loaded[p], ordinal * 16 + 16)
                            for dst, src in halves(0, slot, p):
                                act.copy(dst, src).then_inc(w_hi, 1)

                    def columns(b):
                        for r in range(2):
                            act.wait_ge(transposed, b * 2 + (r + 1))
                            act.copy(xT[0][:, 4 * r:4 * r + 4, :], pt[r][:, :, :]).then_inc(x_hi, 1)

                    def y_out(b):
                        act.wait_ge(y_free, b + 1)
                        for j in range(2):
                            act.wait_ge(down, b * 2 + (j + 3))
                            act.activation(y[:, j, :], py[j][:, :], ACT.Copy, scale=wcol[:, 0:1]).then_inc(y_ready, 1)

                    def sigmoid(b):
                        act.wait_ge(gate_up, b + 1)
                        act.activation(s_[:, :], pgu[:, 0:DE], ACT.Sigmoid).then_inc(sig_done, 1)

                    def hiddens(b):
                        act.wait_ge(h_transposed, b + 1)
                        act.copy(hT[0][:, :, :], ph[:, :, :]).then_inc(h_hi, 1)

                    columns(0)
                    split(0, 0, (0, 1, 2))
                    split(1, 1, (0, 1))
                    sigmoid(0)
                    columns(1)
                    hiddens(0)
                    split(1, 1, (2,))
                    with act.Fori(0, n - 1) as i:
                        following = table(act, self.blk_split, i + 1, NE - 1)
                        slot = following % 2
                        with act.If(following >= 1):
                            split(following, slot, (0, 1))
                        sigmoid(i + 1)
                        columns(i + 2)
                        y_out(i)
                        hiddens(i + 1)
                        with act.If(following >= 1):
                            split(following, slot, (2,))
                    y_out(n - 1)

                @block.vector
                def _(dve):
                    n = blocks_of(dve)

                    def split(ordinal, slot, which):
                        for p, q, (dst, src), (hi, _) in ((p, q, lo, hi) for p in which for q, (lo, hi) in
                                                          enumerate(zip(halves(1, slot, p), halves(0, slot, p)))):
                            dve.wait_ge(w_hi, ordinal * 6 + (2 * p + q + 1))
                            dve.tensor_tensor(dst, src, hi.bitcast(F32), ALU.subtract).then_inc(w_lo, 1)

                    def columns(b):
                        for r in range(2):
                            dve.wait_ge(x_hi, b * 2 + (r + 1))
                            dve.tensor_tensor(xT[1][:, 4 * r:4 * r + 4, :], pt[r][:, :, :], xT[0][:, 4 * r:4 * r + 4, :].bitcast(F32),
                                              ALU.subtract).then_inc(x_lo, 1)

                    def silu(b):
                        dve.wait_ge(sig_done, b + 1)
                        dve.tensor_tensor(s_[:, :], s_[:, :], pgu[:, 0:DE], ALU.mult).then_inc(silu_done, 1)
                        dve.wait_ge(silu_done, b + 1)
                        dve.tensor_tensor(h[:, :], s_[:, :], pgu[:, DE:2 * DE], ALU.mult).then_inc(hidden, 1)

                    def hiddens(b):
                        dve.wait_ge(h_hi, b + 1)
                        dve.tensor_tensor(hT[1][:, :, :], ph[:, :, :], hT[0][:, :, :].bitcast(F32), ALU.subtract).then_inc(h_lo, 1)

                    dve.sem_inc(w_lo, AHEAD)
                    columns(0)
                    split(0, 0, (0, 1, 2))
                    split(1, 1, (0, 1))
                    silu(0)
                    columns(1)
                    hiddens(0)
                    split(1, 1, (2,))
                    with dve.Fori(0, n - 1) as i:
                        following = table(dve, self.blk_split, i + 1, NE - 1)
                        slot = following % 2
                        with dve.If(following >= 1):
                            split(following, slot, (0, 1))
                        silu(i + 1)
                        columns(i + 2)
                        hiddens(i + 1)
                        with dve.If(following >= 1):
                            split(following, slot, (2,))

    def combine(self):
        nc, I, O = self.nc, self.I, self.O
        S = self.sem
        g2_loaded = [S("cb_g2_prompt"), S("cb_g2_sample")]
        gl, sq, ms, rt, gated, x3, o_ready = map(S, ("cb_gain", "cb_sq", "cb_ms", "cb_root", "cb_gated", "cb_x3", "cb_out"))
        y_loaded = [S(f"cb_y{i}") for i in range(4)]
        o_stored = [S("cb_st0"), S("cb_st1")]
        x2 = self.x2
        flat = self.mod_rows.rearrange("r p -> (r p)")
        with ExitStack() as st:
            sb = lambda n, s, d=F32: st.enter_context(nc.sbuf_tensor(n, s, d))
            gain = sb("cb_gainb", [P, D])
            g2b = sb("cb_g2b", [P, 2, D])
            y = sb("cb_y", [P, 4, D])
            junk = sb("cb_junk", [P, D])
            o = sb("cb_o", [P, 2, D])
            ss, m, r, ri = (sb(f"cb_{n}", [P, NT]) for n in ("ss", "m", "r", "ri"))
            with nc.Block() as block:
                @block.sync
                def _(sp):
                    def gate_rows(g):
                        at = (g * 48 + G2 * 8) * P
                        sp.dma_start(g2b[:, g, :], flat[at:at + D].partition_broadcast(P)).then_inc(g2_loaded[g], 16)

                    gate_rows(0)
                    for t in range(NT):
                        R = rows_of(t)
                        if t == 1:
                            sp.dma_start(gain[:, :], I["final_gain"].partition_broadcast(P)).then_inc(gl, 16)
                        if t == 3:
                            gate_rows(1)
                        if t >= 4:
                            sp.wait_ge(x3, t - 3)
                        sp.dma_start(y[:R, t % 4, :], self.sum_rows[t * P:t * P + R, :]).then_inc(y_loaded[t % 4], 16)
                        if t >= 4:
                            self.store_out(sp, t - 4, o, o_ready, o_stored)
                    for t in range(NT - 4, NT):
                        self.store_out(sp, t, o, o_ready, o_stored)
                    sp.wait_ge(o_stored[0], 16 * ((NT + 1) // 2))
                    sp.wait_ge(o_stored[1], 16 * (NT // 2))

                @block.vector
                def _(dve):
                    link = self.link_of(dve, "dve")

                    def out(t):
                        R = rows_of(t)
                        dve.wait_ge(rt, t + 1)
                        link(dve.reciprocal(ri[:R, t:t + 1], r[:R, t:t + 1]))
                        dve.wait_ge(gl, 16)
                        if t >= 2:
                            dve.wait_ge(o_stored[t % 2], 16 * (t // 2))
                        dve.scalar_tensor_tensor(o[:R, t % 2, :], x2[:R, t, :], ri[:R, t:t + 1], gain[:R, :], ALU.mult, ALU.mult).then_inc(o_ready, 1)

                    for t in range(NT):
                        R = rows_of(t)
                        g = int(t == NT - 1)
                        v = y[:R, t % 4, :]
                        dve.wait_ge(g2_loaded[g], 16)
                        dve.wait_ge(y_loaded[t % 4], 16 * (t // 4 + 1))
                        dve.tensor_tensor(v, v, g2b[:R, g, :], ALU.mult).then_inc(gated, 1)
                        dve.wait_ge(gated, t + 1)
                        dve.tensor_tensor(x2[:R, t, :], x2[:R, t, :], v, ALU.add).then_inc(x3, 1)
                        if t:
                            out(t - 1)
                        dve.wait_ge(sq, t + 1)
                        dve.tensor_scalar(m[:R, t:t + 1], ss[:R, t:t + 1], 1.0 / D, EPS, ALU.mult, ALU.add).then_inc(ms, 1)
                    out(NT - 1)

                @block.scalar
                def _(act):
                    link = self.link_of(act, "act")
                    for t in range(NT):
                        R = rows_of(t)
                        act.wait_ge(x3, t + 1)
                        link(act.activation(junk[:R, :], x2[:R, t, :], ACT.Square, accum_out=ss[:R, t:t + 1]))
                        act.sem_inc(sq, 1)
                        act.wait_ge(ms, t + 1)
                        act.activation(r[:R, t:t + 1], m[:R, t:t + 1], ACT.Sqrt).then_inc(rt, 1)

    def store_out(self, sp, t, o, o_ready, o_stored):
        R = rows_of(t)
        dst = self.O["y_prompt"][0, t * P:(t + 1) * P, :] if t < NT - 1 else self.O["y_sample"][0]
        sp.wait_ge(o_ready, t + 1)
        sp.dma_start(dst, o[:R, t % 2, :]).then_inc(o_stored[t % 2], 16)


_OUTS = [("y_prompt", (1, SEQ, D)), ("y_sample", (1, DEC, D)), ("prompt_conv", (1, 1, 2, D)),
         ("prompt_k", (1, 1, WINDOW, NKV, HD)), ("prompt_v", (1, 1, WINDOW, NKV, HD)),
         ("sample_conv", (1, 1, 2, D)), ("sample_k", (1, 1, WINDOW, NKV, HD)), ("sample_v", (1, 1, WINDOW, NKV, HD))]


def kernel(**inputs):
    import numpy as _np
    import concourse.bacc as _bacc
    from concourse.bass_utils import run_bass_kernel_spmd as _run

    nc = _bacc.Bacc("TRN2", target_bir_lowering=False, num_devices=1)
    arrays, ins = {}, {}
    inputs = dict(inputs)
    inputs["con"] = constants()
    for name, value in inputs.items():
        a = _np.ascontiguousarray(value)
        arrays[f"in_{name}"] = a
        ins[name] = nc.dram_tensor(f"in_{name}", a.shape, mybir.dt.from_np(a.dtype), kind="ExternalInput").ap()
    outs = {n: nc.dram_tensor(f"out_{n}", s, F32, kind="ExternalOutput").ap() for n, s in _OUTS}
    Program(nc, ins, outs).build()
    r = _run(nc, [arrays], core_ids=[0])
    return tuple(r.results[0][f"out_{n}"] for n, _ in _OUTS)
```
